# Optimizing a Trainium2 kernel written in Bass

```python
import math
import jax, jax.numpy as jnp
from jax import lax
import numpy as np

D_MODEL = 1024
BATCH = 1
SEQ = 1024
DEPTH = 2

CTX_LEN = 256
GRID_W = 64
N_DN_HEADS = 4
DN_HEAD_DIM = 128
DN_WIDTH = N_DN_HEADS * DN_HEAD_DIM
N_FT_GROUPS = 4
FT_GROUP_DIM = 128
FT_WIDTH = N_FT_GROUPS * FT_GROUP_DIM
MIX_WIDTH = DN_WIDTH + FT_WIDTH
CONV_K = 5
CHUNK = 64
FT_OFF = 4 * DN_WIDTH + 4 * N_DN_HEADS
IN_WIDTH = FT_OFF + FT_WIDTH
N_EXPERTS = 16
N_EXPERT_GROUPS = 4
EXPERTS_PER_GROUP = N_EXPERTS // N_EXPERT_GROUPS
TOP_K = 2
D_EXPERT = 512
MOE_BLOCK = 256
POS_BASE = 10000.0
EPS = 1e-6

kernel_name = "hybrid_deltanet_fourier_moe_dit"

F32 = jnp.float32

def rmsnorm(x, w):
    xf = x.astype(F32)
    y = xf * lax.rsqrt(jnp.mean(xf * xf, axis=-1, keepdims=True) + EPS)
    return (y * w.astype(F32)).astype(x.dtype)

def modulate(h, shift, scale):
    return h * (1.0 + scale) + shift

def l2norm(t):
    return t * lax.rsqrt(jnp.sum(t * t, axis=-1, keepdims=True) + EPS)

def sincos_2d(length, dim, dtype):
    rows = length // GRID_W
    quarter = dim // 4
    omega = 1.0 / (POS_BASE ** (jnp.arange(quarter, dtype=F32) / quarter))
    ang_r = jnp.arange(rows, dtype=F32)[:, None] * omega
    ang_c = jnp.arange(GRID_W, dtype=F32)[:, None] * omega
    emb_r = jnp.concatenate([jnp.sin(ang_r), jnp.cos(ang_r)], axis=-1)
    emb_c = jnp.concatenate([jnp.sin(ang_c), jnp.cos(ang_c)], axis=-1)
    half = dim // 2
    emb = jnp.concatenate([jnp.broadcast_to(emb_r[:, None, :], (rows, GRID_W, half)),
                           jnp.broadcast_to(emb_c[None, :, :], (rows, GRID_W, half))], axis=-1)
    return emb.reshape(rows * GRID_W, dim).astype(dtype)

def short_conv(u, w):
    return lax.conv_general_dilated(u, w[:, None, :].astype(u.dtype), window_strides=(1,), padding='SAME',
                                    dimension_numbers=('NWC', 'WIO', 'NWC'),
                                    feature_group_count=u.shape[-1])

def dn_inputs(p, conv_w, a_log, dt_bias):
    b, l, _ = p.shape
    qkv = jax.nn.silu(short_conv(p[..., :3 * DN_WIDTH], conv_w)).astype(F32)
    q, k, v = jnp.split(qkv, 3, axis=-1)
    heads = lambda t: t.reshape(b, l, N_DN_HEADS, DN_HEAD_DIM).transpose(0, 2, 1, 3)
    q = l2norm(heads(q)) * (DN_HEAD_DIM ** -0.5)
    k = l2norm(heads(k))
    v = heads(v)
    ab = p[..., 4 * DN_WIDTH:FT_OFF].astype(F32).reshape(b, l, 2, 2, N_DN_HEADS)
    g = -jnp.exp(a_log.astype(F32)) * jax.nn.softplus(ab[..., 0, :] + dt_bias.astype(F32))
    beta = jax.nn.sigmoid(ab[..., 1, :])
    return q, k, v, g.transpose(2, 0, 3, 1), beta.transpose(2, 0, 3, 1)

def gated_delta_chunked(q, k, v, g, beta, s0):
    b, h, l, dk = q.shape
    dv = v.shape[-1]
    n = l // CHUNK
    chunks = lambda t: t.reshape(b, h, n, CHUNK, *t.shape[3:])
    q, k, v, g, beta = chunks(q), chunks(k), chunks(v), chunks(g), chunks(beta)
    g = jnp.cumsum(g, axis=-1)
    idx = jnp.arange(CHUNK)
    incl = idx[:, None] >= idx[None, :]
    strict = idx[:, None] > idx[None, :]
    decay = jnp.exp(jnp.where(incl, g[..., :, None] - g[..., None, :], -jnp.inf))
    kb = k * beta[..., None]
    a_mat = jnp.where(strict, jnp.einsum('bhnid,bhnjd->bhnij', kb, k) * decay, 0.0)
    lower = a_mat + jnp.eye(CHUNK, dtype=a_mat.dtype)
    rhs = jnp.concatenate([v * beta[..., None], kb * jnp.exp(g)[..., None]], axis=-1)
    sol = lax.linalg.triangular_solve(lower, rhs, left_side=True, lower=True, unit_diagonal=True)
    u, w = sol[..., :dv], sol[..., dv:]
    qk = jnp.where(incl, jnp.einsum('bhnid,bhnjd->bhnij', q, k) * decay, 0.0)
    q_dec = q * jnp.exp(g)[..., None]
    k_dec = k * jnp.exp(g[..., -1:] - g)[..., None]
    g_end = jnp.exp(g[..., -1])

    def step(s, inp):
        u_i, w_i, q_i, k_i, qk_i, ge_i = inp
        v_new = u_i - jnp.einsum('bhck,bhkv->bhcv', w_i, s)
        o_i = jnp.einsum('bhck,bhkv->bhcv', q_i, s) + jnp.einsum('bhcj,bhjv->bhcv', qk_i, v_new)
        s = s * ge_i[..., None, None] + jnp.einsum('bhck,bhcv->bhkv', k_i, v_new)
        return s, o_i

    xs = tuple(jnp.moveaxis(t, 2, 0) for t in (u, w, q_dec, k_dec, qk, g_end))
    s_fin, o = lax.scan(step, s0, xs)
    o = jnp.moveaxis(o, 0, 2).reshape(b, h, l, dv)
    return o, s_fin

def delta_bidir(q, k, v, g, beta, s0_f, s0_b):
    o_f, s_f = gated_delta_chunked(q, k, v, g[0], beta[0], s0_f)
    flip = lambda t: jnp.flip(t, axis=2)
    o_b, s_b = gated_delta_chunked(flip(q), flip(k), flip(v), flip(g[1]), flip(beta[1]), s0_b)
    return o_f + flip(o_b), s_f, s_b

def dn_output(o, z, norm_w):
    b, h, l, d = o.shape
    o = o.transpose(0, 2, 1, 3)
    o = o * lax.rsqrt(jnp.mean(o * o, axis=-1, keepdims=True) + EPS) * norm_w.astype(F32)
    o = o * jax.nn.silu(z.astype(F32).reshape(b, l, h, d))
    return o.reshape(b, l, h * d).astype(z.dtype)

def fourier_mix(f, norm_w):
    b, l, _ = f.shape
    fg = f.astype(F32).reshape(b, l, N_FT_GROUPS, FT_GROUP_DIM)
    y = jnp.real(jnp.fft.fft2(fg, axes=(1, 3), norm='ortho')).reshape(b, l, FT_WIDTH)
    return rmsnorm(y, norm_w).astype(f.dtype)

def mixer(h_lat, h_ctx, w_in, conv_w, a_log, dt_bias, dn_norm_w, ft_norm_w, w_out, ctx_out):
    p_l = h_lat @ w_in
    p_c = h_ctx @ (w_in if ctx_out else w_in[:, :FT_OFF])
    ql, kl, vl, gl, bl = dn_inputs(p_l, conv_w, a_log, dt_bias)
    qc, kc, vc, gc, bc = dn_inputs(p_c, conv_w, a_log, dt_bias)
    s0 = jnp.zeros((h_ctx.shape[0], N_DN_HEADS, DN_HEAD_DIM, DN_HEAD_DIM), F32)
    o_c, s_f, s_b = delta_bidir(qc, kc, vc, gc, bc, s0, s0)
    o_l, _, _ = delta_bidir(ql, kl, vl, gl, bl, s_f, s_b)

    def merge(p, o):
        dn = dn_output(o, p[..., 3 * DN_WIDTH:4 * DN_WIDTH], dn_norm_w)
        ft = fourier_mix(p[..., FT_OFF:], ft_norm_w)
        return jnp.concatenate([dn, ft], axis=-1) @ w_out

    out_l = merge(p_l, o_l)
    out_c = merge(p_c, o_c) if ctx_out else None
    return out_l, out_c

def moe(h, router_w, router_bias, w_gate, w_up, w_down):
    t, d = h.shape
    scores = jax.nn.sigmoid(h.astype(F32) @ router_w.astype(F32))
    biased = (scores + router_bias.astype(F32)).reshape(t, N_EXPERT_GROUPS, EXPERTS_PER_GROUP)
    group_score = jnp.sum(lax.top_k(biased, 2)[0], axis=-1)
    best_group = jnp.argmax(group_score, axis=-1).astype(jnp.int32)
    in_group = jnp.take_along_axis(biased, best_group[:, None, None], axis=1)[:, 0]
    _, local = lax.top_k(in_group, TOP_K)
    expert_idx = best_group[:, None] * EXPERTS_PER_GROUP + local.astype(jnp.int32)
    wts = jnp.take_along_axis(scores, expert_idx, axis=1)
    wts = wts / jnp.sum(wts, axis=-1, keepdims=True)

    a = t * TOP_K
    flat_e = expert_idx.reshape(a)
    flat_tok = jnp.arange(a, dtype=jnp.int32) // TOP_K
    flat_w = wts.reshape(a).astype(h.dtype)
    order = jnp.argsort(flat_e)
    se = flat_e[order]
    counts = jnp.zeros((N_EXPERTS,), jnp.int32).at[flat_e].add(1)
    padded = (counts + MOE_BLOCK - 1) // MOE_BLOCK * MOE_BLOCK
    pad_end = jnp.cumsum(padded)
    pad_start = pad_end - padded
    start = jnp.cumsum(counts) - counts
    dest = pad_start[se] + (jnp.arange(a, dtype=jnp.int32) - start[se])
    n_blk = (a + N_EXPERTS * (MOE_BLOCK - 1) + MOE_BLOCK - 1) // MOE_BLOCK
    p = n_blk * MOE_BLOCK
    slot_tok = jnp.full((p,), t, jnp.int32).at[dest].set(flat_tok[order])
    slot_w = jnp.zeros((p,), h.dtype).at[dest].set(flat_w[order])
    blk_expert = jnp.minimum(jnp.searchsorted(pad_end, jnp.arange(n_blk, dtype=jnp.int32) * MOE_BLOCK,
                                              side='right'), N_EXPERTS - 1)
    h_pad = jnp.concatenate([h, jnp.zeros((1, d), h.dtype)], axis=0)

    def expert_block(args):
        tok, gate, e = args
        xb = h_pad[tok]
        hid = jax.nn.silu(xb @ w_gate[e]) * (xb @ w_up[e])
        return (hid @ w_down[e]) * gate[:, None]

    ys = lax.map(expert_block, (slot_tok.reshape(n_blk, MOE_BLOCK), slot_w.reshape(n_blk, MOE_BLOCK), blk_expert))
    return jax.ops.segment_sum(ys.reshape(p, d), slot_tok, num_segments=t + 1)[:t]

def setup_inputs(seed: int = 0) -> dict:
    key = jax.random.key(seed)
    ks = jax.random.split(key, 21)
    nrm = lambda k, shape, s: jax.random.normal(k, shape, F32) * s
    x = nrm(ks[0], (BATCH, SEQ, D_MODEL), 1.0)
    c = nrm(ks[1], (BATCH, D_MODEL), 1.0)
    ctx = nrm(ks[2], (BATCH, CTX_LEN, D_MODEL), 1.0)
    c_ctx = nrm(ks[3], (D_MODEL,), 1.0)
    ada_w = nrm(ks[4], (DEPTH, D_MODEL, 6 * D_MODEL), 0.5 * D_MODEL ** -0.5)
    ada_b = nrm(ks[5], (DEPTH, 6 * D_MODEL), 0.02)
    norm_mix_w = 1.0 + nrm(ks[6], (DEPTH, D_MODEL), 0.02)
    norm_ffn_w = 1.0 + nrm(ks[7], (DEPTH, D_MODEL), 0.02)
    w_in = nrm(ks[8], (DEPTH, D_MODEL, IN_WIDTH), D_MODEL ** -0.5)
    conv_w = nrm(ks[9], (DEPTH, CONV_K, 3 * DN_WIDTH), CONV_K ** -0.5)
    a_log = jnp.log(jax.random.uniform(ks[10], (DEPTH, 2, N_DN_HEADS), F32, 1.0, 16.0))
    dt = jnp.exp(jax.random.uniform(ks[11], (DEPTH, 2, N_DN_HEADS), F32, math.log(1e-3), math.log(1e-1)))
    dt_bias = dt + jnp.log(-jnp.expm1(-dt))
    dn_norm_w = 1.0 + nrm(ks[12], (DEPTH, DN_HEAD_DIM), 0.02)
    ft_norm_w = 1.0 + nrm(ks[13], (DEPTH, FT_WIDTH), 0.02)
    w_out = nrm(ks[14], (DEPTH, MIX_WIDTH, D_MODEL), MIX_WIDTH ** -0.5)
    router_w = nrm(ks[15], (D_MODEL, N_EXPERTS), D_MODEL ** -0.5)
    router_bias = nrm(ks[16], (N_EXPERTS,), 0.01)
    w_gate = nrm(ks[17], (DEPTH, N_EXPERTS, D_MODEL, D_EXPERT), D_MODEL ** -0.5)
    w_up = nrm(ks[18], (DEPTH, N_EXPERTS, D_MODEL, D_EXPERT), D_MODEL ** -0.5)
    w_down = nrm(ks[19], (DEPTH, N_EXPERTS, D_EXPERT, D_MODEL), D_EXPERT ** -0.5)
    final_norm_w = 1.0 + nrm(ks[20], (D_MODEL,), 0.02)
    return {"x": x, "c": c, "ctx": ctx, "c_ctx": c_ctx, "ada_w": ada_w, "ada_b": ada_b,
            "norm_mix_w": norm_mix_w, "norm_ffn_w": norm_ffn_w, "w_in": w_in, "conv_w": conv_w,
            "a_log": a_log, "dt_bias": dt_bias, "dn_norm_w": dn_norm_w, "ft_norm_w": ft_norm_w,
            "w_out": w_out, "router_w": router_w, "router_bias": router_bias, "w_gate": w_gate,
            "w_up": w_up, "w_down": w_down, "final_norm_w": final_norm_w}

def reference(x, c, ctx, c_ctx, ada_w, ada_b, norm_mix_w, norm_ffn_w, w_in, conv_w, a_log, dt_bias,
              dn_norm_w, ft_norm_w, w_out, router_w, router_bias, w_gate, w_up, w_down, final_norm_w):
    b, l, d = x.shape
    lc = ctx.shape[1]
    xl = x + sincos_2d(l, d, x.dtype)[None]
    xc = ctx
    c_act = jax.nn.silu(c)
    cc_act = jax.nn.silu(c_ctx)
    for i in range(DEPTH):
        last = i == DEPTH - 1
        mod_l = (c_act @ ada_w[i] + ada_b[i])[:, None, :]
        mod_c = (cc_act @ ada_w[i] + ada_b[i])[None, None, :]
        sh1, sc1, g1, sh2, sc2, g2 = jnp.split(mod_l, 6, axis=-1)
        sh1c, sc1c, g1c, sh2c, sc2c, g2c = jnp.split(mod_c, 6, axis=-1)

        hl = modulate(rmsnorm(xl, norm_mix_w[i]), sh1, sc1)
        hc = modulate(rmsnorm(xc, norm_mix_w[i]), sh1c, sc1c)
        ol, oc = mixer(hl, hc, w_in[i], conv_w[i], a_log[i], dt_bias[i], dn_norm_w[i], ft_norm_w[i],
                       w_out[i], not last)
        xl = xl + g1 * ol
        hl2 = modulate(rmsnorm(xl, norm_ffn_w[i]), sh2, sc2)
        if last:
            y = moe(hl2.reshape(b * l, d), router_w, router_bias, w_gate[i], w_up[i], w_down[i])
            xl = xl + g2 * y.reshape(b, l, d)
        else:
            xc = xc + g1c * oc
            hc2 = modulate(rmsnorm(xc, norm_ffn_w[i]), sh2c, sc2c)
            tokens = jnp.concatenate([hl2.reshape(b * l, d), hc2.reshape(b * lc, d)], axis=0)
            y = moe(tokens, router_w, router_bias, w_gate[i], w_up[i], w_down[i])
            xl = xl + g2 * y[:b * l].reshape(b, l, d)
            xc = xc + g2c * y[b * l:].reshape(b, lc, d)
    return rmsnorm(xl, final_norm_w)


_drawn_inputs = setup_inputs


def setup_inputs(seed=0):
    import zlib

    import numpy as np

    out = dict(_drawn_inputs(seed))
    spreads = {}
    factors = {'ctx': 2.916,
     'c_ctx': 4.319,
     'norm_mix_w': 2.975,
     'dn_norm_w': 4.621,
     'ft_norm_w': 19.132,
     'final_norm_w': 8.778,
     'norm_ffn_w': 5.014}
    for name, (base, spread) in spreads.items():
        noise = np.random.default_rng([zlib.crc32(name.encode()), seed]).standard_normal(out[name].shape)
        drawn = base * np.exp(spread * noise) if base else spread * noise
        out[name] = __import__('jax').numpy.asarray(drawn.astype(out[name].dtype))
    for name, factor in factors.items():
        out[name] = (out[name] * factor).astype(out[name].dtype)
    return out
```

```python
from contextlib import ExitStack

import concourse.bass as bass
from concourse import mybir

F32 = mybir.dt.float32
I32 = mybir.dt.int32
U32 = mybir.dt.uint32
ALU = mybir.AluOpType
ACT = mybir.ActivationFunctionType
X_AXIS = mybir.AxisListType.X

P = 128
D = 1024
KD = D // P
SEQ = 1024
CTX = 256
NCT = CTX // P
NLT = SEQ // P
NT = NCT + NLT
DEPTH = 2
NH = 4
HW = NH * P
CONV_K = 5
PADC = CONV_K // 2
AB_OFF = 4 * HW
FT_OFF = AB_OFF + 4 * NH
MODS = 6 * D
NE = 16
NG = 4
EPG = NE // NG
DE = 512
KE = DE // P
EPS = 1e-6
LEVELS = 7
CHUNK_POS = NT + NCT
LAT, CTXV = 0, 1
BANK = 512


def ceil_even(n):
    return n + n % 2


def max_blocks(tokens):
    return ceil_even((2 * tokens + NE * (P - 1)) // P)


def heads(ap, n=NH):
    return ap.rearrange("p (h c) -> p h c", h=n)


def over_cols(ap, n, c=P):
    return ap.unsqueeze(2).broadcast_to([P, n, c])


def over_heads(ap, n=NH):
    return ap.unsqueeze(1).broadcast_to([P, n, ap.shape[1]])


class Memory:

    def __init__(self, nc, stack):
        self.nc, self.stack = nc, stack
        self.X = self.sb("X", [P, NT, D])
        self.ident = self.sb("ident", [P, P])
        self.upto = self.sb("upto", [P, 2, P])
        self.after = self.sb("after", [P, 2, P])
        self.ones = self.sb("ones", [P, P])
        self.levels = self.sb("levels", [P, 2, LEVELS, P])
        self.cdsd = self.sb("cdsd", [P, 2 * P])
        self.logits = self.sb("logits", [P, NT, NE])
        self.d0i, self.d1i = self.sb("d0i", [P, NT], U32), self.sb("d1i", [P, NT], U32)
        self.w0, self.w1 = self.sb("w0", [P, NT]), self.sb("w1", [P, NT])
        self.blk_tok = self.sb("blk_tok", [P, max_blocks(NT * P)], I32)
        self.buffer, self.loads0, self.loads1 = (self.sb(x, [1, max_blocks(NT * P)], I32) for x in ("buffer", "loads0", "loads1"))
        self.even, self.odd = (self.sb(x, [1, NE + 2], I32) for x in ("even", "odd"))
        self.a1, self.b1 = self.sb("a1", [P, 2, KD]), self.sb("b1", [P, 2, KD])
        self.pairs_but_one = self.sb("pairs", [1, 1], I32)

    def sb(self, name, shape, dt=F32):
        return self.stack.enter_context(self.nc.sbuf_tensor(name, shape, dt))


def phase(nc, tag):
    stack, sems = ExitStack(), []

    def clear():
        nc.clear_and_free_semaphores(sems)
        nc.all_engine_barrier()
    stack.callback(clear)

    def sb(name, shape, dt=F32):
        return stack.enter_context(nc.sbuf_tensor(f"{tag}_{name}", shape, dt))

    def banks(n):
        return [stack.enter_context(nc.psum_tensor(f"{tag}_bank{i}", [P, BANK], F32)) for i in range(n)]

    def sem(name):
        sems.append(nc.alloc_semaphore(name=f"{tag}_{name}"))
        return sems[-1]

    return stack, sb, banks, sem


def credit(eng, *sems):
    for s in sems:
        eng.sem_inc(s, 1)


def load_start(nc, m, g):
    stack, sb, banks, sem = phase(nc, "start")
    with stack:
        emb_c = sb("emb_c", [P, D // 2])
        emb_r = sb("emb_r", [P, NLT, D // 2])
        loaded, rows, const, added = sem("loaded"), sem("rows"), sem("const"), sem("added")
        mod = Modulation(nc, m, g, 0, sb, banks(3), sem)
        block = stack.enter_context(nc.Block())

        @block.sync
        def _(sp):
            mod.load(sp)
            mod.store(sp)

        @block.scalar
        def _(act):
            mod.load_small(act)
            for dst, src in ((m.ident[:, :], g.consts[:, 0:P]),
                             (m.upto[:, :, :], g.consts[:, P:3 * P]),
                             (m.after[:, :, :], g.consts[:, 3 * P:5 * P]),
                             (m.ones[:, :], g.consts[:, 5 * P:6 * P]),
                             (m.cdsd[:, :], g.consts[:, 6 * P:8 * P]),
                             (m.levels[:, :, :, :], g.consts[:, 8 * P:(8 + 2 * LEVELS) * P])):
                act.dma_start(dst, src).then_inc(const, 16)
            for t in range(NT):
                src = g.ctx[0] if t < NCT else g.x[0]
                r = (t if t < NCT else t - NCT) * P
                act.dma_start(m.X[:, t, :], src[r:r + P, :]).then_inc(loaded, 16)
            act.dma_start(emb_c[:, :], g.emb_col).then_inc(loaded, 16)
            for t in range(NLT):
                for half in range(2):
                    act.dma_start(emb_r[half * 64:half * 64 + 64, t, :],
                                  g.emb_row[2 * t + half, :].partition_broadcast(64)).then_inc(rows, 16)
            mod.take(act)
            act.wait_ge(const, 6 * 16)

        @block.vector
        def _(dve):
            dve.wait_ge(loaded, 16 * (NT + 1))
            dve.wait_ge(rows, 16 * 2 * NLT)
            for t in range(NLT):
                xt = m.X[:, NCT + t, :]
                nc.vector.tensor_tensor(xt[:, 0:D // 2], xt[:, 0:D // 2], emb_r[:, t, :], ALU.add).then_inc(added, 1)
                nc.vector.tensor_tensor(xt[:, D // 2:D], xt[:, D // 2:D], emb_c[:, :], ALU.add).then_inc(added, 1)
            mod.finish(dve)

        @block.tensor
        def _(pe):
            mod.products(pe)
            pe.wait_ge(const, 6 * 16)
            mod.turn(pe)


class Modulation:

    def __init__(self, nc, m, g, layer, sb, ps, sem):
        self.nc, self.m, self.g, self.layer, self.ps = nc, m, g, layer, ps
        self.craw = sb("mod_craw", [P, 2, KD])
        self.cact = sb("mod_cact", [P, 2, KD])
        self.w = sb("mod_w", [P, 2, KD, BANK])
        self.row = sb("mod_row", [2, MODS])
        self.bias = sb("mod_bias", [2, MODS])
        self.nw = sb("mod_nw", [P, KD])
        self.c_loaded, self.bias_loaded, self.act_done, self.biased, self.turned, self.a_plus, self.stored, self.ab_done = (
            sem(f"mod_{x}") for x in ("c_loaded", "bias_loaded", "act_done", "biased", "turned", "a_plus", "stored", "ab_done"))
        self.w_loaded, self.prod, self.row_done = (
            [sem(f"mod_{x}{j}") for j in range(2)] for x in ("w_loaded", "prod", "row_done"))
        self.CHUNKS = MODS // BANK
        self.FIRST = 2 * D

    def load(self, sp):
        g, layer = self.g, self.layer
        for v in (LAT, CTXV):
            sp.dma_start(self.craw[:, v, :], g.c_cols[:, 0 if v == LAT else 1, :]).then_inc(self.c_loaded, 16)
        with sp.Fori(0, self.CHUNKS // 2) as i:
            for j in range(2):
                sp.wait_ge(self.prod[j], i + 1)
                sp.dma_start(self.w[:, j, :, :], g.ada_w[layer][:, bass.ds((i * 2 + j) * BANK, BANK)].rearrange(
                    "(k p) n -> p k n", p=P)).then_inc(self.w_loaded[j], 16)

    def store(self, sp):
        sp.wait_ge(self.biased, 2)
        sp.dma_start(self.g.mods[self.layer], self.row[:, :]).then_inc(self.stored, 16)
        sp.wait_ge(self.stored, 16)

    def load_small(self, act):
        g, layer = self.g, self.layer
        for r in range(2):
            act.dma_start(self.bias[r:r + 1, :], g.ada_b[layer:layer + 1, :]).then_inc(self.bias_loaded, 16)
        act.dma_start(self.nw[:, :], g.norm_mix_cols[layer]).then_inc(self.bias_loaded, 16)

    def take(self, act):
        nc = self.nc
        credit(act, *self.row_done)
        act.wait_ge(self.c_loaded, 32)
        nc.scalar.activation(self.cact[:, :, :], self.craw[:, :, :], ACT.Silu).then_inc(self.act_done, 1)
        with act.Fori(0, self.CHUNKS // 2) as i:
            for j in range(2):
                act.wait_ge(self.prod[j], i + 2)
                nc.scalar.activation(self.row[:, bass.ds((i * 2 + j) * BANK, BANK)], self.ps[j][0:2, :],
                                     ACT.Copy).then_inc(self.row_done[j], 1)

    def products(self, pe):
        nc = self.nc
        credit(pe, *self.prod)
        pe.wait_ge(self.act_done, 1)
        with pe.Fori(0, self.CHUNKS // 2) as i:
            for j in range(2):
                pe.wait_ge(self.w_loaded[j], i * 16 + 16)
                pe.wait_ge(self.row_done[j], i + 1)
                for k in range(KD):
                    mm = nc.tensor.matmul(self.ps[j][0:2, :], self.cact[:, :, k], self.w[:, j, k, :], start=(k == 0), stop=(k == KD - 1))
                mm.then_inc(self.prod[j], 1)

    def turn(self, pe):
        nc = self.nc
        pe.wait_ge(self.biased, 1)
        for q in range(2 * KD):
            tr = nc.tensor.transpose(self.ps[2][:, 2 * q:2 * q + 2], self.row[0:2, q * P:(q + 1) * P], self.m.ident[0:2, 0:2])
        tr.then_inc(self.turned, 1)

    def finish(self, dve):
        nc, m = self.nc, self.m
        dve.wait_ge(self.bias_loaded, 48)
        for j in range(2):
            dve.wait_ge(self.row_done[j], self.CHUNKS // 2 + 1)
        for c in (slice(0, self.FIRST), slice(self.FIRST, MODS)):
            nc.vector.tensor_tensor(self.row[:, c], self.row[:, c], self.bias[:, c], ALU.add).then_inc(self.biased, 1)
        dve.wait_ge(self.turned, 1)
        cols = self.ps[2][:, 0:4 * KD].rearrange("p (s k v) -> p s v k", s=2, v=2)
        for v in range(2):
            nc.vector.tensor_copy(m.b1[:, v, :], cols[:, 0, v, :]).then_inc(self.ab_done, 1)
            nc.vector.tensor_scalar(m.a1[:, v, :], cols[:, 1, v, :], 1.0, None, ALU.add).then_inc(self.a_plus, 1)
        dve.wait_ge(self.a_plus, 2)
        for v in range(2):
            nc.vector.tensor_tensor(m.a1[:, v, :], m.a1[:, v, :], self.nw[:, :], ALU.mult).then_inc(self.ab_done, 1)


def token_projections(nc, m, g, layer):
    stack, sb, banks, sem = phase(nc, f"tok{layer}")
    with stack:
        WZ, WF, WA = 0, HW, 2 * HW
        w = sb("w", [P, KD, 2 * HW + 4 * NH])
        junk = sb("junk", [P, D])
        ss = sb("ss", [P, NT])
        rs = sb("rs", [P, 2])
        xn = sb("xn", [P, KD, P])
        hs = sb("hs", [P, 2, KD, P])
        fs = sb("fs", [P, NH, P])
        gc = sb("gc", [P, 2, NH, P])
        ps = banks(7)
        wz_loaded, w_loaded, squared, meaned, rooted = sem("wz_loaded"), sem("w_loaded"), sem("squared"), sem("meaned"), sem("rooted")
        inverted, rs_copied, xn_done = sem("inverted"), sem("rs_copied"), sem("xn_done")
        turned, hs_done, h_copied = sem("turned"), sem("hs_done"), sem("h_copied")
        z_prod, z_out, f_prod, f_out, ab_prod, ab_out = (sem(n) for n in ("z_prod", "z_out", "f_prod", "f_out", "ab_prod", "ab_out"))
        dft, gc_act, gc_dve, gc_stored = sem("dft"), sem("gc_act"), sem("gc_dve"), sem("gc_stored")
        block = stack.enter_context(nc.Block())
        assert NCT == 2 and NT % 2 == 0

        def loop(eng, body):
            with eng.Fori(0, (NT - 2) // 2) as i:
                for j in range(2):
                    body(i * 2 + (j + 1), i * 2 + j, 1 - j)

        @block.sync
        def _(sp):
            wi = g.w_in[layer].rearrange("(k p) n -> p k n", p=P)
            for loaded, dst, src, n in ((wz_loaded, WZ, 3 * HW, HW), (w_loaded, WF, FT_OFF, HW), (w_loaded, WA, AB_OFF, 4 * NH)):
                for k in range(0, KD, 4):
                    sp.dma_start(w[:, k:k + 4, dst:dst + n], wi[:, k:k + 4, src:src + n]).then_inc(loaded, 16)

            def store(t):
                sp.wait_ge(gc_act, t + 2)
                sp.wait_ge(gc_dve, t + 2)
                sp.dma_start(g.dft1[bass.ds(t, 1), :, :].rearrange("t p n -> p (t n)"),
                             gc[:, :, :, :].rearrange("p a h c -> p (a h c)")).then_inc(gc_stored, 16)
            with sp.Fori(0, NT) as t:
                store(t)
            sp.wait_ge(gc_stored, 16 * NT + 16)

        @block.gpsimd
        def _(pool):
            with pool.Fori(0, NT // 2) as i:
                for j in range(2):
                    pool.wait_ge(hs_done, i * 4 + 2 * j + 2)
                    nc.gpsimd.tensor_copy(m.hT[:, :, bass.ds((i * 2 + j) * P, P)], hs[:, j, :, :]).then_inc(h_copied, 1)

        @block.scalar
        def _(act):
            credit(act, z_out, gc_act, squared)
            with act.Fori(0, NT) as t:
                act.wait_ge(squared, t + 1)
                nc.scalar.activation(junk[:, :], m.X[:, bass.ds(t, 1), :].rearrange("p a n -> p (a n)"), ACT.Square,
                                     accum_out=ss[:, bass.ds(t, 1)]).then_inc(squared, 1)
            act.wait_ge(meaned, 1)
            nc.scalar.activation(ss[:, :], ss[:, :], ACT.Sqrt).then_inc(rooted, 1)

            def modulate(t, buffer, vec):
                act.wait_ge(turned, t * 2 + 1)
                act.wait_ge(h_copied, t)
                act.wait_ge(ab_prod, t)
                for k in range(KD // 2):
                    a = nc.scalar.activation(hs[:, buffer, k, :], ps[0][:, k * P:(k + 1) * P], ACT.Identity,
                                             bias=m.b1[:, vec, k:k + 1], scale=m.a1[:, vec, k:k + 1])
                a.then_inc(hs_done, 1)

            def silu_z(t):
                act.wait_ge(z_prod, t + 1)
                nc.scalar.activation(m.Z[:, bass.ds(t, 1), :].rearrange("p a n -> p (a n)"), ps[2][:, :],
                                     ACT.Silu).then_inc(z_out, 1)

            def dft_out(t):
                act.wait_ge(dft, t * 2 + 1)
                act.wait_ge(gc_stored, t * 16 + 16)
                nc.scalar.activation(gc[:, :, 0:2, :].rearrange("p a h c -> p h a c"),
                                     ps[5][:, :].rearrange("p (h a c) -> p h a c", h=2, a=2), ACT.Copy).then_inc(gc_act, 1)

            def body(t, u, buffer):
                silu_z(t)
                dft_out(u)
                modulate(t + 1, 1 - buffer, LAT)
            modulate(0, 0, CTXV)
            silu_z(0)
            modulate(1, 1, CTXV)
            loop(act, body)
            silu_z(NT - 1)
            dft_out(NT - 2)
            dft_out(NT - 1)

        @block.vector
        def _(dve):
            credit(dve, f_out, ab_out, gc_dve, h_copied, ab_prod)
            dve.sem_inc(gc_stored, 16)
            dve.wait_ge(squared, NT + 1)
            nc.vector.tensor_scalar(ss[:, :], ss[:, :], 1.0 / D, EPS, ALU.mult, ALU.add).then_inc(meaned, 1)
            dve.wait_ge(rooted, 1)
            nc.vector.reciprocal(ss[:, :], ss[:, :]).then_inc(inverted, 1)
            dve.wait_ge(inverted, 1)

            def normalise(t):
                if not isinstance(t, int) or t > 0:
                    dve.wait_ge(turned, t * 2)
                nc.vector.tensor_copy(rs[:, 0:1], ss[:, bass.ds(t, 1)]).then_inc(rs_copied, 1)
                dve.wait_ge(rs_copied, t + 1)
                nc.vector.tensor_scalar(xn[:, :, :].rearrange("p k c -> p (k c)"),
                                        m.X[:, bass.ds(t, 1), :].rearrange("p a n -> p (a n)"),
                                        rs[:, 0:1], None, ALU.mult).then_inc(xn_done, 1)

            def modulate(t, buffer, vec):
                dve.wait_ge(turned, t * 2 + 2)
                dve.wait_ge(h_copied, t)
                dve.wait_ge(ab_prod, t)
                for k in range(KD // 2, KD):
                    a = nc.vector.tensor_scalar(hs[:, buffer, k, :], ps[1][:, (k - 4) * P:(k - 3) * P], m.a1[:, vec, k:k + 1],
                                                m.b1[:, vec, k:k + 1], ALU.mult, ALU.add)
                a.then_inc(hs_done, 1)

            def take_products(t):
                dve.wait_ge(f_prod, t + 1)
                nc.vector.tensor_copy(fs[:, :, :].rearrange("p h c -> p (h c)"), ps[3][:, :]).then_inc(f_out, 1)
                dve.wait_ge(ab_prod, t + 2)
                nc.vector.tensor_copy(m.AB[:, bass.ds(t, 1), :].rearrange("p a n -> p (a n)"),
                                      ps[4][:, 0:4 * NH]).then_inc(ab_out, 1)

            def dft_out(t):
                dve.wait_ge(dft, t * 2 + 2)
                dve.wait_ge(gc_stored, t * 16 + 16)
                nc.vector.tensor_copy(gc[:, :, 2:4, :].rearrange("p a h c -> p h a c"),
                                      ps[6][:, :].rearrange("p (h a c) -> p h a c", h=2, a=2)).then_inc(gc_dve, 1)

            def body(t, u, buffer):
                normalise(t + 1)
                dft_out(u)
                modulate(t + 1, 1 - buffer, LAT)
                take_products(t)
            normalise(0)
            modulate(0, 0, CTXV)
            normalise(1)
            modulate(1, 1, CTXV)
            take_products(0)
            loop(dve, body)
            dft_out(NT - 2)
            take_products(NT - 1)
            dft_out(NT - 1)

        @block.tensor
        def _(pe):
            def turn(t):
                pe.wait_ge(xn_done, t + 1)
                for half in range(2):
                    for k in range(4):
                        tr = nc.tensor.transpose(ps[half][:, k * P:(k + 1) * P], xn[:, half * 4 + k, :], m.ident[:, :])
                    tr.then_inc(turned, 1)

            def z(t, buffer):
                pe.wait_ge(hs_done, t * 2 + 2)
                pe.wait_ge(z_out, t + 1)
                for k in range(KD):
                    mm = nc.tensor.matmul(ps[2][:, :], hs[:, buffer, k, :], w[:, k, WZ:WZ + HW], start=(k == 0), stop=(k == KD - 1))
                mm.then_inc(z_prod, 1)

            def f_ab(t, buffer):
                pe.wait_ge(f_out, t + 1)
                for h in range(NH):
                    for k in range(KD):
                        mm = nc.tensor.matmul(ps[3][:, h * P:(h + 1) * P], w[:, k, WF + h * P:WF + (h + 1) * P], hs[:, buffer, k, :],
                                              start=(k == 0), stop=(k == KD - 1))
                mm.then_inc(f_prod, 1)
                pe.wait_ge(ab_out, t + 1)
                for k in range(KD):
                    mm = nc.tensor.matmul(ps[4][:, 0:4 * NH], hs[:, buffer, k, :], w[:, k, WA:WA + 4 * NH], start=(k == 0),
                                          stop=(k == KD - 1))
                mm.then_inc(ab_prod, 1)

            def dft_features(t):
                pe.wait_ge(f_out, t + 2)
                pe.wait_ge(gc_act, t + 1)
                pe.wait_ge(gc_dve, t + 1)
                for half in range(2):
                    for h in range(2):
                        mm = nc.tensor.matmul(ps[5 + half][:, h * 2 * P:(h + 1) * 2 * P], fs[:, half * 2 + h, :],
                                              m.cdsd[:, :], start=True, stop=True)
                    mm.then_inc(dft, 1)

            def body(t, u, buffer):
                z(t, buffer)
                dft_features(u)
                turn(t + 1)
                f_ab(t, buffer)
            turn(0)
            pe.wait_ge(wz_loaded, 2 * 16)
            z(0, 0)
            turn(1)
            pe.wait_ge(w_loaded, 4 * 16)
            f_ab(0, 0)
            loop(pe, body)
            z(NT - 1, 1)
            dft_features(NT - 2)
            f_ab(NT - 1, 1)
            dft_features(NT - 1)


def feature_projections(nc, m, g, layer):
    stack, sb, banks, sem = phase(nc, f"feat{layer}")
    with stack:
        NF = 3 * NH
        PADDED = CTX + SEQ + 4 * PADC
        WIDE = PADDED - 2 * PADC
        LAT_AT = CTX + 2 * PADC
        GROUPS = ((0, 0, CTX), (LAT_AT, CTX, BANK), (LAT_AT + BANK, CTX + BANK, BANK))
        w = sb("w", [P, 2, KD, P])
        cw = sb("cw", [P, NF, CONV_K])
        taps = sb("taps", [P, 2, CONV_K])
        eps = sb("eps", [P, 1])
        padded, acc, s, sq, r = (sb(n, [P, 2, PADDED]) for n in ("padded", "acc", "s", "sq", "r"))
        ps = banks(6)

        def pair(name):
            return [sem(f"{name}0"), sem(f"{name}1")]
        w_loaded, prod, evacuated, conv, silu, squared = (pair(n) for n in ("w_loaded", "prod", "evacuated", "conv", "silu", "squared"))
        normed, rooted, inverted, scaled, stored, tapped, tap = (pair(n) for n in ("normed", "rooted", "inverted", "scaled", "stored", "tapped", "tap"))
        cw_loaded, cleared = sem("cw_loaded"), sem("cleared")
        block = stack.enter_context(nc.Block())
        lag_loop = 3

        @block.sync
        def _(sp):
            sp.dma_start(cw[:, :, :], g.conv_cols[layer]).then_inc(cw_loaded, 16)
            with sp.Fori(0, NF // 2) as i:
                for j in range(2):
                    sp.wait_ge(prod[j], i + 1)
                    sp.dma_start(w[:, j, :, :], g.w_in[layer][:, bass.ds((i * 2 + j) * P, P)].rearrange(
                        "(k p) n -> p k n", p=P)).then_inc(w_loaded[j], 16)

        @block.tensor
        def _(pe):
            credit(pe, *prod)

            def product(j, n, freed):
                pe.wait_ge(w_loaded[j], n * 16 + 16)
                pe.wait_ge(freed[j], n + 1)
                for b, (at, col, width) in enumerate(GROUPS):
                    for k in range(KD):
                        mm = nc.tensor.matmul(ps[3 * j + b][:, 0:width], w[:, j, k, :], m.hT[:, k, col:col + width],
                                              start=(k == 0), stop=(k == KD - 1))
                mm.then_inc(prod[j], 1)

            def norm(j, n):
                pe.wait_ge(squared[j], n + 1)
                for b, (at, col, width) in enumerate(GROUPS):
                    mm = nc.tensor.matmul(ps[3 * j + b][:, 0:width], m.ones[:, :], sq[:, j, at:at + width], start=True, stop=True)
                mm.then_inc(normed[j], 1)
            product(0, 0, rooted)
            with pe.Fori(0, lag_loop) as i:
                product(1, i, rooted)
                norm(0, i)
                product(0, i + 1, rooted)
                norm(1, i)
            product(1, 3, rooted)
            norm(0, 3)
            product(0, 4, rooted)
            norm(1, 3)
            product(1, 4, rooted)
            product(0, 5, evacuated)
            product(1, 5, evacuated)

        @block.scalar
        def _(act):
            credit(act, *rooted, *evacuated)
            act.wait_ge(cleared, 2)

            def evacuate(j, n):
                act.wait_ge(prod[j], n + 2)
                act.wait_ge(conv[j], n + 1)
                for b, (at, col, width) in enumerate(GROUPS):
                    a = nc.scalar.activation(padded[:, j, PADC + at:PADC + at + width], ps[3 * j + b][:, 0:width], ACT.Copy)
                a.then_inc(evacuated[j], 1)

            def gate(j, n):
                act.wait_ge(conv[j], n + 2)
                act.wait_ge(stored[j], n * 48 + 48)
                nc.scalar.activation(s[:, j, 0:WIDE], acc[:, j, 0:WIDE], ACT.Silu).then_inc(silu[j], 1)

            def square(j, n):
                act.wait_ge(silu[j], n + 1)
                nc.scalar.activation(sq[:, j, 0:WIDE], s[:, j, 0:WIDE], ACT.Square).then_inc(squared[j], 1)

            def root(j, n):
                act.wait_ge(normed[j], n + 1)
                for b, (at, col, width) in enumerate(GROUPS):
                    a = nc.scalar.activation(r[:, j, at:at + width], ps[3 * j + b][:, 0:width], ACT.Sqrt, bias=eps[:, 0:1])
                a.then_inc(rooted[j], 1)

            def store(j, n, ready):
                act.wait_ge(ready[j], n + 1)
                for at, pos, width in ((0, 0, CTX), (LAT_AT, CTX, SEQ), (0, CTX + SEQ, CTX)):
                    act.dma_start(g.qkv[bass.ds(n * 2 + j, 1), :, pos:pos + width].rearrange("f p c -> p (f c)"),
                                  s[:, j, at:at + width]).then_inc(stored[j], 16)
            evacuate(0, 0)
            gate(0, 0)
            square(0, 0)
            with act.Fori(0, lag_loop) as i:
                evacuate(1, i)
                root(0, i)
                gate(1, i)
                square(1, i)
                store(0, i, scaled)
                evacuate(0, i + 1)
                root(1, i)
                gate(0, i + 1)
                square(0, i + 1)
                store(1, i, scaled)
            evacuate(1, 3)
            root(0, 3)
            gate(1, 3)
            square(1, 3)
            store(0, 3, scaled)
            evacuate(0, 4)
            root(1, 3)
            gate(0, 4)
            store(1, 3, scaled)
            store(0, 4, silu)
            for j, n in ((1, 4), (0, 5), (1, 5)):
                evacuate(j, n)
                gate(j, n)
                store(j, n, silu)
            for j in range(2):
                act.wait_ge(stored[j], 48 * (NF // 2 + 1))

        @block.vector
        def _(dve):
            credit(dve, *conv)
            for j in range(2):
                dve.sem_inc(stored[j], 48)
            nc.vector.memset(padded[:, :, :], 0.0).then_inc(cleared, 1)
            nc.vector.memset(r[:, :, :], 1.0).then_inc(cleared, 1)
            nc.vector.memset(eps[:, :], EPS).then_inc(cleared, 1)
            dve.wait_ge(cleared, 3)
            dve.wait_ge(cw_loaded, 16)

            def convolve(j, n):
                dve.wait_ge(evacuated[j], n + 2)
                nc.vector.tensor_copy(taps[:, j, :], cw[:, bass.ds(n * 2 + j, 1), :].rearrange("p a k -> p (a k)")).then_inc(tapped[j], 1)
                dve.wait_ge(tapped[j], n + 1)
                for k in range(CONV_K):
                    src, out = padded[:, j, k:k + WIDE], acc[:, j, 0:WIDE]
                    if k == 0:
                        a = nc.vector.tensor_scalar(out, src, taps[:, j, k:k + 1], None, ALU.mult)
                    else:
                        dve.wait_ge(tap[j], n * (CONV_K - 1) + k)
                        a = nc.vector.scalar_tensor_tensor(out=out, in0=src, scalar=taps[:, j, k:k + 1], in1=out,
                                                           op0=ALU.mult, op1=ALU.add)
                    a.then_inc(tap[j] if k < CONV_K - 1 else conv[j], 1)

            def scale(j, n):
                dve.wait_ge(rooted[j], n + 2)
                nc.vector.reciprocal(r[:, j, 0:WIDE], r[:, j, 0:WIDE]).then_inc(inverted[j], 1)
                dve.wait_ge(inverted[j], n + 1)
                nc.vector.tensor_tensor(s[:, j, 0:WIDE], s[:, j, 0:WIDE], r[:, j, 0:WIDE], ALU.mult).then_inc(scaled[j], 1)
            convolve(0, 0)
            with dve.Fori(0, lag_loop) as i:
                convolve(1, i)
                scale(0, i)
                convolve(0, i + 1)
                scale(1, i)
            convolve(1, 3)
            scale(0, 3)
            convolve(0, 4)
            scale(1, 3)
            for j, n in ((1, 4), (0, 5), (1, 5)):
                convolve(j, n)


def fourier(nc, m, g, layer, last):
    stack, sb, banks, sem = phase(nc, f"four{layer}")
    with stack:
        K = 2 * NLT
        f1 = sb("f1", [P, K, HW])
        cs = sb("cs", [P, 2, K, P])
        nw = sb("nw", [P, HW])
        junk = sb("junk", [P, 2, HW])
        ss = sb("ss", [P, 2])
        ps = banks(4)

        def pair(name):
            return [sem(f"{name}0"), sem(f"{name}1")]
        cs_loaded, prod, squared, meaned, rooted, inverted, done = (
            pair(n) for n in ("cs_loaded", "prod", "squared", "meaned", "rooted", "inverted", "done"))
        QUARTERS = 4
        f_loaded, nw_loaded = [sem(f"f_loaded{q}") for q in range(QUARTERS)], sem("nw_loaded")
        if not last:
            fc = sb("fc", [P, 2 * NCT, HW])
            csc = sb("csc", [P, 2 * NCT, CTX])
            c_loaded = sem("c_loaded")
        block = stack.enter_context(nc.Block())
        NS = NLT // 2

        @block.sync
        def _(sp):
            with sp.Fori(0, NS) as i:
                for j in range(2):
                    sp.wait_ge(prod[j], i + 1)
                    sp.dma_start(cs[:, j, :, :], g.dft_lat[:, bass.ds((i * 2 + j) * P, P)].rearrange(
                        "(k p) n -> p k n", p=P)).then_inc(cs_loaded[j], 16)
            if not last:
                for part in range(2):
                    sp.dma_start(fc[:, part * NCT:(part + 1) * NCT, :],
                                 g.dft1[0:NCT, :, part * HW:(part + 1) * HW].rearrange("t p n -> p t n")).then_inc(c_loaded, 16)
                sp.dma_start(csc[:, :, :], g.dft_ctx.rearrange("(k p) n -> p k n", p=P)).then_inc(c_loaded, 16)

        @block.tensor
        def _(pe):
            credit(pe, *prod)
            with pe.Fori(0, NS) as i:
                for j in range(2):
                    pe.wait_ge(cs_loaded[j], i * 16 + 16)
                    pe.wait_ge(done[j], i + 1)
                    for k in range(K):
                        if j == 0 and k % (K // QUARTERS) == 0:
                            pe.wait_ge(f_loaded[k // (K // QUARTERS)], 16)
                        mm = nc.tensor.matmul(ps[j][:, :], cs[:, j, k, :], f1[:, k, :], start=(k == 0), stop=(k == K - 1))
                    mm.then_inc(prod[j], 1)
            if not last:
                pe.wait_ge(c_loaded, 48)
                for j in range(NCT):
                    pe.wait_ge(done[j], NS + 1)
                    for k in range(2 * NCT):
                        mm = nc.tensor.matmul(ps[j][:, :], csc[:, k, j * P:(j + 1) * P], fc[:, k, :], start=(k == 0),
                                              stop=(k == 2 * NCT - 1))
                    mm.then_inc(prod[j], 1)

        @block.scalar
        def _(act):
            for q in range(QUARTERS):
                part, t = divmod(q * K // QUARTERS, NLT)
                act.dma_start(f1[:, q * K // QUARTERS:(q + 1) * K // QUARTERS, :],
                              g.dft1[NCT + t:NCT + t + K // QUARTERS, :, part * HW:(part + 1) * HW].rearrange(
                                  "t p n -> p t n")).then_inc(f_loaded[q], 16)
            act.dma_start(nw[:, :], g.ft_norm_w[layer].partition_broadcast(P)).then_inc(nw_loaded, 16)

            def stats(j, n):
                act.wait_ge(prod[j], n + 2)
                act.wait_ge(done[j], n + 1)
                nc.scalar.activation(junk[:, j, :], ps[j][:, :], ACT.Square, accum_out=ss[:, j:j + 1]).then_inc(squared[j], 1)
                act.wait_ge(meaned[j], n + 1)
                nc.scalar.activation(ss[:, j:j + 1], ss[:, j:j + 1], ACT.Sqrt).then_inc(rooted[j], 1)
            with act.Fori(0, NS) as i:
                stats(0, i)
                stats(1, i)
            if not last:
                stats(0, NS)
                stats(1, NS)

        @block.vector
        def _(dve):
            credit(dve, *done)
            dve.wait_ge(nw_loaded, 16)

            def scale(j, n, tile):
                dve.wait_ge(squared[j], n + 1)
                nc.vector.tensor_scalar(ss[:, j:j + 1], ss[:, j:j + 1], 1.0 / HW, EPS, ALU.mult, ALU.add).then_inc(meaned[j], 1)
                dve.wait_ge(rooted[j], n + 1)
                nc.vector.reciprocal(ss[:, j:j + 1], ss[:, j:j + 1]).then_inc(inverted[j], 1)
                dve.wait_ge(inverted[j], n + 1)
                nc.vector.scalar_tensor_tensor(out=m.F[:, bass.ds(tile, 1), :].rearrange("p a n -> p (a n)"), in0=ps[j][:, :],
                                               scalar=ss[:, j:j + 1], in1=nw[:, :], op0=ALU.mult, op1=ALU.mult).then_inc(done[j], 1)
            with dve.Fori(0, NS) as i:
                scale(0, i, i * 2 + NCT)
                scale(1, i, i * 2 + NCT + 1)
            if not last:
                scale(0, NS, 0)
                scale(1, NS, 1)


def delta(nc, m, g, layer):
    stack, sb, banks, sem = phase(nc, f"delta{layer}")
    with stack:
        GB = sb("GB", [P, CHUNK_POS, 2, 2, NH])
        nega = sb("nega", [P, 2, NH])
        dtb = sb("dtb", [P, 2, NH])
        tmp = sb("tmp", [P, NT, 2, NH])
        tmp2 = sb("tmp2", [P, NT, 2, NH])
        qkv = sb("qkv", [P, 2, 3, NH, P])

        def wide(*names):
            return [sb(n, [P, 2, HW]) for n in names]
        q2, gm, gl, E, Eb, ET, ETm, A = wide("q2", "gm", "gl", "E", "Eb", "ET", "ETm", "A")
        am0, am1, T, U, Zs, kbe, kdec, vb = wide("am0", "am1", "T", "U", "Zs", "kbe", "kdec", "vb")
        qkm, wn, vn, o, S, Sg = wide("qkm", "wn", "vn", "o", "S", "Sg")
        Am = (am0, am1)
        gs = sb("gs", [P, 2, 2, NH])
        eg = sb("eg", [P, 2, 3, NH])
        be = sb("be", [P, 2, NH])
        ps = banks(8)
        bA, bB, bC, bD = ps[0:2], ps[2:4], ps[4:6], ps[6:8]

        def pair(name):
            return [sem(f"{name}0"), sem(f"{name}1")]
        loaded, gs_r, gm_r, gl_r, de, et_ps, cum = (pair(n) for n in ("loaded", "gs", "gm", "gl", "de", "et_ps", "cum"))
        e_r, et_r, eg_r, q2_r, kk, ktr, vtr, qk = (pair(n) for n in ("e", "et", "eg", "q2", "kk", "ktr", "vtr", "qk"))
        be_r, eb_r, etm_r, a_r, kbe_r, kdec_r, vb_r, qkm_r = (
            pair(n) for n in ("be", "eb", "etm", "a", "kbe", "kdec", "vb", "qkm"))
        am_r, atr, t_r, u_r, z, zs_r, up, tp = (pair(n) for n in ("am", "atr", "t", "u", "z", "zs", "up", "tp"))
        w_ps, wn_r, vn_ps, vn_r, os_ps, oi_ps, kv_ps = (pair(n) for n in ("w_ps", "wn", "vn_ps", "vn", "os", "oi", "kv"))
        o1_r, o_r, s_r, sg_r, stored = (pair(n) for n in ("o1", "o", "s", "sg", "stored"))
        params, gates = sem("params"), sem("gates")
        gate_act = sem("gate_act")
        spare = range(2 * NT, max_blocks(NT * P))
        nothing = sb("nothing", [P, D])
        cleared_tile, cleared = sem("cleared_tile"), sem("cleared")
        block = stack.enter_context(nc.Block())
        G_PARAMS, G_SUM, G_ABS, G_ONE, G_LOG, G_G, G_B1, G_BETA, G_ALL = 1, 2, 3, 4, 5, 6, 7, 8, 9
        L1 = LEVELS - 1
        NEXT_STAGES = (2, 3, 5, 6)
        NEXT_E, NEXT_ET = 3, 4

        def changing(ap, d, l):
            size = 1 << l
            return ap.rearrange("p (b t s) -> p b t s", t=2, s=size)[:, :, 1 - d, :]

        def turned_cols(ap, d, l):
            size = 1 << l
            return ap.rearrange("p (b t s) -> p b t s", t=2, s=size)[:, :, d, :]

        def compact(ap, l):
            return ap.rearrange("p (b s) -> p b s", s=1 << l)

        def position(i, d):
            return i if d == 0 else i * -1 + (CHUNK_POS - 1)

        @block.sync
        def _(sp):
            sp.dma_start(nega[:, :, :], g.a_log[layer].partition_broadcast(P)).then_inc(params, 16)
            sp.dma_start(dtb[:, :, :], g.dt_bias[layer].partition_broadcast(P)).then_inc(params, 16)
            if layer == 0:
                sp.wait_ge(cleared_tile, 1)
                for b in spare:
                    sp.dma_start(g.ys[b * P:(b + 1) * P, :], nothing[:, :]).then_inc(cleared, 16)
            with sp.Fori(0, NT) as i:
                for d in range(2):
                    sp.wait_ge(o_r[d], i + 2)
                    sp.dma_start(g.o[d][bass.ds(position(i, d), 1), :, :].rearrange("c p n -> p (c n)"), o[:, d, :]).then_inc(stored[d], 16)
            for d in range(2):
                sp.wait_ge(stored[d], 16 * NT + 16)
            if layer == 0:
                sp.wait_ge(cleared, 16 * len(spare))

        @block.gpsimd
        def _(pool):
            def gates_of(c):
                for d in range(2):
                    pool.wait_ge(vb_r[d], c + 1)
                    nc.gpsimd.tensor_copy(gs[:, d, :, :], GB[:, bass.ds(position(c, d), 1), d, :, :].rearrange(
                        "p a s h -> p (a s) h")).then_inc(gs_r[d], 1)
                for d in range(2):
                    pool.wait_ge(gs_r[d], c + 1)
                    nc.gpsimd.tensor_tensor(heads(gm[:, d, :]), over_heads(m.after[:, d, :]), over_cols(gs[:, d, 0, :], NH),
                                            ALU.mult).then_inc(gm_r[d], 1)

            def gates_upto(c):
                for d in range(2):
                    nc.gpsimd.tensor_tensor(heads(gl[:, d, :]), over_heads(m.upto[:, d, :]), over_cols(gs[:, d, 0, :], NH),
                                            ALU.mult).then_inc(gl_r[d], 1)

            def beta_decay(c):
                for d in range(2):
                    pool.wait_ge(e_r[d], c + 1)
                    nc.gpsimd.tensor_tensor(heads(Eb[:, d, :]), heads(E[:, d, :]), over_cols(gs[:, d, 1, :], NH),
                                            ALU.mult).then_inc(eb_r[d], 1)

            def masked_decay(c):
                for d in range(2):
                    pool.wait_ge(et_r[d], c + 1)
                    nc.gpsimd.tensor_tensor(heads(ETm[:, d, :]), heads(ET[:, d, :]), over_heads(m.upto[:, d, :]),
                                            ALU.mult).then_inc(etm_r[d], 1)
            pool.wait_ge(gates, G_ALL)
            for stage in (gates_of, gates_upto, beta_decay, masked_decay):
                stage(0)
            with pool.Fori(0, NT) as i:
                for l in range(LEVELS):
                    for d in range(2):
                        if l == 0:
                            pool.wait_ge(a_r[d], i + 1)
                        elif l == 2:
                            pool.wait_ge(atr[d], i + 1)
                            pool.wait_ge(t_r[d], i * L1 + 1)
                        elif l > 2:
                            pool.wait_ge(z[d], i * L1 + l - 2)
                        nc.gpsimd.tensor_tensor(heads(Am[l % 2][:, d, :]), heads(A[:, d, :]), over_heads(m.levels[:, d, l, :]),
                                                ALU.mult).then_inc(am_r[d], 1)
                        if l == 0:
                            pool.wait_ge(am_r[d], i * LEVELS + 1)
                            nc.gpsimd.tensor_tensor(heads(T[:, d, :]), over_heads(m.ident[:, :]), heads(am0[:, d, :]),
                                                    ALU.subtract).then_inc(t_r[d], 1)
                    if l in NEXT_STAGES:
                        (gates_of, gates_upto, beta_decay, masked_decay)[NEXT_STAGES.index(l)](i + 1)
                for d in range(2):
                    pool.wait_ge(eg_r[d], i + 1)
                    pool.wait_ge(s_r[d], i + 1)
                    nc.gpsimd.tensor_tensor(heads(Sg[:, d, :]), heads(S[:, d, :]), over_cols(eg[:, d, 2, :], NH),
                                            ALU.mult).then_inc(sg_r[d], 1)

        @block.scalar
        def _(act):
            def load(pos, d):
                act.dma_start(qkv[:, d, :, :, :].rearrange("p s h c -> p (s h) c"),
                              g.qkv[:, :, bass.ds(pos * P, P)].rearrange("f p c -> p f c")).then_inc(loaded[d], 16)
            for d in range(2):
                load(position(0, d), d)
            act.wait_ge(params, 32)
            nc.scalar.activation(nega[:, :, :], nega[:, :, :], ACT.Exp).then_inc(gate_act, 1)
            act.wait_ge(gates, G_ABS)
            nc.scalar.activation(tmp2[:, :, :, :], tmp2[:, :, :, :], ACT.Exp, scale=-1.0).then_inc(gate_act, 1)
            act.wait_ge(gates, G_ONE)
            nc.scalar.activation(tmp2[:, :, :, :], tmp2[:, :, :, :], ACT.Ln).then_inc(gate_act, 1)
            act.wait_ge(gates, G_G)
            nc.scalar.activation(tmp[:, :, :, :], m.AB[:, :, :].rearrange("p t (d s h) -> p t d s h", d=2, s=2)[:, :, :, 1, :],
                                 ACT.Exp, scale=-1.0).then_inc(gate_act, 1)

            def exp_e(c):
                for d in range(2):
                    act.wait_ge(de[d], c + 1)
                    nc.scalar.activation(E[:, d, :], bD[d][:, :], ACT.Exp).then_inc(e_r[d], 1)

            def exp_et(c):
                for d in range(2):
                    act.wait_ge(et_ps[d], c + 1)
                    nc.scalar.activation(ET[:, d, :], bD[d][:, :], ACT.Exp).then_inc(et_r[d], 1)
            exp_e(0)
            exp_et(0)
            with act.Fori(0, NT) as i:
                for d in range(2):
                    act.wait_ge(loaded[d], i * 16 + 16)
                    act.wait_ge(os_ps[d], i + 1)
                    nc.scalar.activation(q2[:, d, :], qkv[:, d, 0, :, :].rearrange("p h c -> p (h c)"), ACT.Copy,
                                         scale=float(P) ** -0.5).then_inc(q2_r[d], 1)
                for d in range(2):
                    act.wait_ge(cum[d], i + 1)
                    act.wait_ge(o1_r[d], i + 1)
                    act.wait_ge(sg_r[d], i + 1)
                    nc.scalar.activation(eg[:, d, :, :].rearrange("p s h -> p (s h)"), bC[d][:, 0:3 * NH], ACT.Exp).then_inc(eg_r[d], 1)
                for l in range(1, LEVELS):
                    for d in range(2):
                        act.wait_ge(z[d], i * L1 + l)
                        nc.scalar.activation(Zs[:, d, 0:HW // 2], bA[d][:, 0:HW // 2], ACT.Copy).then_inc(zs_r[d], 1)
                    if l == NEXT_E:
                        exp_e(i + 1)
                    elif l == NEXT_ET:
                        exp_et(i + 1)
                    if l < L1:
                        for d in range(2):
                            act.wait_ge(tp[d], i * (L1 - 1) + l)
                            nc.scalar.activation(turned_cols(T[:, d, :], d, l), turned_cols(bB[d][:, :], d, l),
                                                 ACT.Copy).then_inc(t_r[d], 1)
                    if l == 1:
                        for d in range(2):
                            act.wait_ge(qk[d], i + 1)
                            load(position(i + 1, d), d)
                for d in range(2):
                    act.wait_ge(w_ps[d], i + 1)
                    nc.scalar.mul(wn[:, d, :], bA[d][:, :], -1.0).then_inc(wn_r[d], 1)
                for d in range(2):
                    act.wait_ge(vn_ps[d], i + 1)
                    nc.scalar.activation(vn[:, d, :], bC[d][:, :], ACT.Copy).then_inc(vn_r[d], 1)
            for d in range(2):
                act.wait_ge(loaded[d], 16 * NT + 16)

        @block.vector
        def _(dve):
            nc.vector.memset(nothing[:, :], 0.0).then_inc(cleared_tile, 1)
            credit(dve, *vb_r, *os_ps, *o1_r, *sg_r, *o_r, *vn_r)
            for d in range(2):
                dve.sem_inc(stored[d], 16)
            ab = m.AB[:, :, :].rearrange("p t (d s h) -> p t d s h", d=2, s=2)

            def over_tiles(ap):
                return ap.unsqueeze(1).broadcast_to([P, NT, 2, NH])
            dve.wait_ge(gate_act, 1)
            nc.vector.tensor_scalar(nega[:, :, :], nega[:, :, :], -1.0, None, ALU.mult).then_inc(gates, 1)
            nc.vector.tensor_tensor(tmp[:, :, :, :], ab[:, :, :, 0, :], over_tiles(dtb[:, :, :]), ALU.add).then_inc(gates, 1)
            dve.wait_ge(gates, G_SUM)
            flat, flat2 = (t[:, :, :, :].rearrange("p t d h -> p (t d h)") for t in (tmp, tmp2))
            nc.vector.scalar_tensor_tensor(out=flat2, in0=flat, scalar=-1.0, in1=flat, op0=ALU.mult, op1=ALU.max).then_inc(gates, 1)
            dve.wait_ge(gate_act, 2)
            nc.vector.tensor_scalar(tmp2[:, :, :, :], tmp2[:, :, :, :], 1.0, None, ALU.add).then_inc(gates, 1)
            dve.wait_ge(gate_act, 3)
            nc.vector.scalar_tensor_tensor(out=flat, in0=flat, scalar=0.0, in1=flat2, op0=ALU.max, op1=ALU.add).then_inc(gates, 1)
            dve.wait_ge(gates, G_LOG)
            nc.vector.tensor_tensor(GB[:, 0:NT, :, 0, :], tmp[:, :, :, :], over_tiles(nega[:, :, :]), ALU.mult).then_inc(gates, 1)
            dve.wait_ge(gate_act, 4)
            nc.vector.tensor_scalar(tmp2[:, :, :, :], tmp[:, :, :, :], 1.0, None, ALU.add).then_inc(gates, 1)
            dve.wait_ge(gates, G_B1)
            nc.vector.reciprocal(GB[:, 0:NT, :, 1, :], tmp2[:, :, :, :]).then_inc(gates, 1)
            dve.wait_ge(gates, G_BETA)
            nc.vector.tensor_copy(GB[:, NT:CHUNK_POS, :, :, :].rearrange("p t d s h -> p (t d s h)"),
                                  GB[:, 0:NCT, :, :, :].rearrange("p t d s h -> p (t d s h)")).then_inc(gates, 1)
            for d in range(2):
                nc.vector.memset(S[:, d, :], 0.0).then_inc(s_r[d], 1)
            with dve.Fori(0, NT) as i:
                def key_scales(d):
                    dve.wait_ge(ktr[d], i + 1)
                    dve.wait_ge(be_r[d], i + 1)
                    nc.vector.tensor_tensor(heads(kbe[:, d, :]), heads(bD[d][:, :]), over_cols(be[:, d, :], NH), ALU.mult).then_inc(kbe_r[d], 1)
                    nc.vector.tensor_tensor(heads(kdec[:, d, :]), heads(bD[d][:, :]), over_cols(eg[:, d, 1, :], NH), ALU.mult).then_inc(kdec_r[d], 1)
                for d in range(2):
                    dve.wait_ge(kk[d], i + 1)
                    dve.wait_ge(eb_r[d], i + 1)
                    nc.vector.tensor_tensor(A[:, d, :], bA[d][:, :], Eb[:, d, :], ALU.mult).then_inc(a_r[d], 1)
                for d in range(2):
                    dve.wait_ge(eg_r[d], i + 1)
                    nc.vector.tensor_tensor(be[:, d, :], gs[:, d, 1, :], eg[:, d, 0, :], ALU.mult).then_inc(be_r[d], 1)
                key_scales(0)
                for d in range(2):
                    dve.wait_ge(atr[d], i + 1)
                    nc.vector.tensor_tensor(heads(U[:, d, :]), over_heads(m.ident[:, :]), heads(bA[d][:, :]), ALU.subtract).then_inc(u_r[d], 1)
                for d in range(2):
                    dve.wait_ge(vtr[d], i + 1)
                    nc.vector.tensor_tensor(heads(vb[:, d, :]), heads(bC[d][:, :]), over_cols(gs[:, d, 1, :], NH), ALU.mult).then_inc(vb_r[d], 1)
                for d in range(2):
                    dve.wait_ge(qk[d], i + 1)
                    dve.wait_ge(etm_r[d], i + 1)
                    nc.vector.tensor_tensor(qkm[:, d, :], bB[d][:, :], ETm[:, d, :], ALU.mult).then_inc(qkm_r[d], 1)
                key_scales(1)
                for l in range(1, LEVELS):
                    for d in range(2):
                        dve.wait_ge(up[d], i * L1 + l)
                        nc.vector.tensor_tensor(changing(U[:, d, :], d, l), changing(U[:, d, :], d, l),
                                                compact(bC[d][:, 0:HW // 2], l), ALU.subtract).then_inc(u_r[d], 1)
                for d in range(2):
                    dve.wait_ge(os_ps[d], i + 2)
                    dve.wait_ge(stored[d], i * 16 + 16)
                    nc.vector.tensor_tensor(heads(o[:, d, :]), heads(bD[d][:, :]), over_cols(eg[:, d, 0, :], NH), ALU.mult).then_inc(o1_r[d], 1)
                for d in range(2):
                    dve.wait_ge(oi_ps[d], i + 1)
                    dve.wait_ge(o1_r[d], i + 2)
                    nc.vector.tensor_tensor(o[:, d, :], o[:, d, :], bA[d][:, :], ALU.add).then_inc(o_r[d], 1)
                    dve.wait_ge(kv_ps[d], i + 1)
                    dve.wait_ge(sg_r[d], i + 2)
                    nc.vector.tensor_tensor(S[:, d, :], Sg[:, d, :], bB[d][:, :], ALU.add).then_inc(s_r[d], 1)

        @block.tensor
        def _(pe):
            def per_head(out, lhsT, rhs, sem_out, transpose=False):
                for h in range(NH):
                    c = slice(h * P, (h + 1) * P)
                    if transpose:
                        mm = nc.tensor.transpose(out[:, c], lhsT(h, c), m.ident[:, :])
                    else:
                        mm = nc.tensor.matmul(out[:, c], lhsT(h, c), rhs(h, c), start=True, stop=True)
                mm.then_inc(sem_out, 1)

            def per_half(out, lhsT, rhs, sem_out):
                for h in range(NH):
                    c, hc = slice(h * P, (h + 1) * P), slice(h * P // 2, (h + 1) * P // 2)
                    mm = nc.tensor.matmul(out[:, hc], lhsT(h, c), rhs(h, c, hc), start=True, stop=True)
                mm.then_inc(sem_out, 1)

            def sum_e(c):
                for d in range(2):
                    pe.wait_ge(gm_r[d], c + 1)
                    nc.tensor.matmul(bD[d][:, :], m.upto[:, d, :], gm[:, d, :], start=True, stop=True).then_inc(de[d], 1)

            def sum_et(c):
                for d in range(2):
                    pe.wait_ge(gl_r[d], c + 1)
                    pe.wait_ge(e_r[d], c + 1)
                    nc.tensor.matmul(bD[d][:, :], m.after[:, d, :], gl[:, d, :], start=True, stop=True).then_inc(et_ps[d], 1)
            sum_e(0)
            sum_et(0)
            with pe.Fori(0, NT) as i:
                def chunk(n, d):
                    return lambda h, c: qkv[:, d, n, h, :]
                for d in range(2):
                    pe.wait_ge(loaded[d], i * 16 + 16)
                    pe.wait_ge(o_r[d], i + 1)
                    per_head(bA[d], chunk(1, d), chunk(1, d), kk[d])
                for d in range(2):
                    pe.wait_ge(o1_r[d], i + 1)
                    pe.wait_ge(et_r[d], i + 1)
                    per_head(bD[d], chunk(1, d), None, ktr[d], transpose=True)
                for d in range(2):
                    pe.wait_ge(gs_r[d], i + 1)
                    pe.wait_ge(vn_r[d], i + 1)
                    for s, mat in enumerate((m.upto[:, d, :], m.after[:, d, :], m.ones[:, :])):
                        mm = nc.tensor.matmul(bC[d][:, s * NH:(s + 1) * NH], mat, gs[:, d, 0, :], start=True, stop=True)
                    mm.then_inc(cum[d], 1)
                for d in range(2):
                    pe.wait_ge(am_r[d], i * LEVELS + 1)
                    pe.wait_ge(a_r[d], i + 1)
                    per_head(bA[d], lambda h, c: am0[:, d, c], None, atr[d], transpose=True)
                for d in range(2):
                    pe.wait_ge(eg_r[d], i + 1)
                    per_head(bC[d], chunk(2, d), None, vtr[d], transpose=True)
                for d in range(2):
                    pe.wait_ge(s_r[d], i + 1)
                    pe.wait_ge(q2_r[d], i + 1)
                    per_head(bB[d], chunk(1, d), lambda h, c: q2[:, d, c], qk[d])
                for l in range(1, LEVELS):
                    for d in range(2):
                        pe.wait_ge(am_r[d], i * LEVELS + l + 1)
                        pe.wait_ge(u_r[d], i * LEVELS + l)
                        if l > 1:
                            pe.wait_ge(zs_r[d], i * L1 + l - 1)
                        per_half(bA[d], lambda h, c: Am[l % 2][:, d, c], lambda h, c, hc: changing(U[:, d, c], d, l), z[d])
                    for d in range(2):
                        pe.wait_ge(zs_r[d], i * L1 + l)
                        pe.wait_ge(t_r[d], i * L1 + l)
                        if l == 1:
                            pe.wait_ge(vb_r[d], i + 2)
                        per_half(bC[d], lambda h, c: T[:, d, c], lambda h, c, hc: Zs[:, d, hc], up[d])
                    if l == NEXT_E:
                        for d in range(2):
                            pe.wait_ge(kdec_r[d], i + 1)
                        sum_e(i + 1)
                    elif l == NEXT_ET:
                        sum_et(i + 1)
                    if l < L1:
                        for d in range(2):
                            if l == 1:
                                pe.wait_ge(qkm_r[d], i + 1)
                            pe.wait_ge(u_r[d], i * LEVELS + l + 1)
                            per_head(bB[d], lambda h, c: U[:, d, c], None, tp[d], transpose=True)
                for d in range(2):
                    pe.wait_ge(u_r[d], i * LEVELS + LEVELS)
                    pe.wait_ge(kbe_r[d], i + 1)
                    per_head(bA[d], lambda h, c: kbe[:, d, c], lambda h, c: U[:, d, c], w_ps[d])
                for d in range(2):
                    pe.wait_ge(et_r[d], i + 2)
                    pe.wait_ge(s_r[d], i + 1)
                    per_head(bD[d], lambda h, c: q2[:, d, c], lambda h, c: S[:, d, c], os_ps[d])
                    pe.wait_ge(wn_r[d], i + 1)
                    for h in range(NH):
                        c = slice(h * P, (h + 1) * P)
                        nc.tensor.matmul(bC[d][:, c], U[:, d, c], vb[:, d, c], start=True, stop=False)
                        mm = nc.tensor.matmul(bC[d][:, c], wn[:, d, c], S[:, d, c], start=False, stop=True)
                    mm.then_inc(vn_ps[d], 1)
                for d in range(2):
                    pe.wait_ge(vn_r[d], i + 2)
                    per_head(bA[d], lambda h, c: qkm[:, d, c], lambda h, c: vn[:, d, c], oi_ps[d])
                    pe.wait_ge(t_r[d], i * L1 + L1)
                    per_head(bB[d], lambda h, c: kdec[:, d, c], lambda h, c: vn[:, d, c], kv_ps[d])


def output_projection(nc, m, g, layer, n):
    stack, sb, banks, sem = phase(nc, f"out{layer}")
    with stack:
        MIX = 2 * HW
        vecs = 2 if n > NLT else 1
        g1 = sb("g1", [P, vecs, D])
        a2 = sb("a2", [P, vecs, D])
        b2 = sb("b2", [P, vecs, D])
        w_out = sb("w_out", [P, KD, D])
        fw = sb("fw", [P, D])
        nw = sb("nw", [P, P])
        rw = sb("rw", [P, KD, NE])
        ofb = sb("ofb", [P, 2, HW])
        osum, zn, fst, mixed, junk = (sb(x, [P, HW]) for x in ("osum", "zn", "fst", "mixed", "junk"))
        mixT = sb("mixT", [P, KD, P])
        tmp, h2, junk2 = (sb(x, [P, D]) for x in ("tmp", "h2", "junk2"))
        h2T = sb("h2T", [P, KD, P])
        ss, s2 = sb("ss", [P, NH]), sb("s2", [P, 1])
        ps = banks(7)
        const, a2_plus, a2_r, loaded, osum_r, zn_r, fst_r = (sem(x) for x in ("const", "a2_plus", "a2", "loaded", "osum", "zn", "fst"))
        squared, meaned, rooted, inverted, on_r, mixed_r = (sem(x) for x in ("squared", "meaned", "rooted", "inverted", "on", "mixed"))
        turned, mixT_r, prod, tmp_r, x_r = (sem(x) for x in ("turned", "mixT", "prod", "tmp", "x"))
        squared2, meaned2, rooted2, inverted2, xn_r, h2_r, stored = (
            sem(x) for x in ("squared2", "meaned2", "rooted2", "inverted2", "xn", "h2", "stored"))
        turned2, h2T_act, h2T_dve, logits, logits_r = (sem(x) for x in ("turned2", "h2T_act", "h2T_dve", "logits_ps", "logits"))
        block = stack.enter_context(nc.Block())
        nw_loaded, w_loaded = sem("nw_loaded"), sem("w_loaded")

        def vec(r):
            return 1 if isinstance(r, int) and r >= NLT else 0

        def tile_at(r):
            return r - NLT if isinstance(r, int) and r >= NLT else r + NCT

        def back_at(r):
            return tile_at(r) + (CHUNK_POS - NCT if isinstance(r, int) and r >= NLT else 0)

        def staged(eng, mix, update, route, take=None, prepare=None):
            def tail(before, r):
                if take:
                    take(r)
                route(before)
                update(r)
            mix(0)
            mix(1)
            if prepare:
                prepare()
            if take:
                take(0)
            update(0)
            with eng.Fori(0, NLT - 2) as q:
                mix(q + 2)
                tail(q, q + 1)
            for r in range(NLT - 1, n - 1):
                mix(r + 1)
                tail(r - 1, r)
            tail(n - 2, n - 1)
            route(n - 1)

        def tile_of(t, r):
            return t[:, bass.ds(tile_at(r), 1), :].rearrange("p a n -> p (a n)")

        @block.sync
        def _(sp):
            def load(r):
                sp.wait_ge(osum_r, r + 1)
                sp.dma_start(ofb[:, 0, :], g.o[0][bass.ds(tile_at(r), 1), :, :].rearrange("c p n -> p (c n)")).then_inc(loaded, 16)
                sp.dma_start(ofb[:, 1, :], g.o[1][bass.ds(back_at(r), 1), :, :].rearrange("c p n -> p (c n)")).then_inc(loaded, 16)

            def store(r):
                sp.wait_ge(h2_r, r + 1)
                sp.dma_start(g.h2[bass.ds(tile_at(r) * P, P), :], h2[:, :]).then_inc(stored, 16)
            sp.dma_start(nw[:, :], g.dn_norm_w[layer].partition_broadcast(P)).then_inc(nw_loaded, 16)
            load(0)
            w = g.w_out[layer].rearrange("(k p) n -> p k n", p=P)
            for k in range(0, KD, 4):
                sp.dma_start(w_out[:, k:k + 4, :], w[:, k:k + 4, :]).then_inc(w_loaded, 16)
            for v, row in ((0, LAT), (1, CTXV))[:vecs]:
                for dst, off in ((g1, 2), (b2, 3), (a2, 4)):
                    sp.dma_start(dst[:, v, :], g.mods[layer, row, off * D:(off + 1) * D].partition_broadcast(P)).then_inc(const, 16)
            sp.dma_start(fw[:, :], g.norm_ffn_w[layer].partition_broadcast(P)).then_inc(const, 16)
            sp.dma_start(rw[:, :, :], g.router_w.rearrange("(k p) e -> p k e", p=P)).then_inc(const, 16)
            load(1)
            with sp.Fori(0, NLT - 2) as r:
                load(r + 2)
                store(r)
            for r in range(NLT - 2, n):
                if r + 2 < n:
                    load(r + 2)
                store(r)
            sp.wait_ge(stored, 16 * n + 16)

        CONST = 16 * (3 * vecs + 2)

        @block.gpsimd
        def _(pool):
            pool.wait_ge(nw_loaded, 16)

            def mix(r):
                pool.wait_ge(loaded, r * 32 + 32)
                pool.wait_ge(on_r, r + 1)
                nc.gpsimd.tensor_tensor(osum[:, :], ofb[:, 0, :], ofb[:, 1, :], ALU.add).then_inc(osum_r, 1)
                pool.wait_ge(mixed_r, r + 1)
                nc.gpsimd.tensor_tensor(heads(zn[:, :]), tile_of(m.Z, r).rearrange("p (h c) -> p h c", h=NH),
                                        over_heads(nw[:, :]), ALU.mult).then_inc(zn_r, 1)
                pool.wait_ge(turned, r + 1)
                nc.gpsimd.tensor_copy(fst[:, :], tile_of(m.F, r)).then_inc(fst_r, 1)

            def update(r):
                pool.wait_ge(tmp_r, r + 2)
                nc.gpsimd.tensor_tensor(tile_of(m.X, r), tile_of(m.X, r), tmp[:, :], ALU.add).then_inc(x_r, 1)
                pool.wait_ge(xn_r, r + 1)
                nc.gpsimd.tensor_tensor(h2[:, :], h2[:, :], b2[:, vec(r), :], ALU.add).then_inc(h2_r, 1)
            staged(pool, mix, update, lambda r: None)

        @block.scalar
        def _(act):
            credit(act, mixT_r, h2T_act)

            def mix(r):
                act.wait_ge(osum_r, r + 2)
                act.wait_ge(inverted, r + 1)
                act.wait_ge(squared, r + 1)
                for h in range(NH):
                    a = nc.scalar.activation(junk[:, h * P:(h + 1) * P], osum[:, h * P:(h + 1) * P], ACT.Square,
                                             accum_out=ss[:, h:h + 1])
                a.then_inc(squared, 1)
                act.wait_ge(meaned, r + 1)
                nc.scalar.activation(ss[:, :], ss[:, :], ACT.Sqrt).then_inc(rooted, 1)
                act.wait_ge(turned, r + 2)
                act.wait_ge(prod, r + 1)
                for half in range(2):
                    a = nc.scalar.activation(mixT[:, half * NH:(half + 1) * NH, :].rearrange("p k c -> p (k c)"), ps[half][:, :],
                                             ACT.Copy)
                a.then_inc(mixT_r, 1)

            def update(r):
                act.wait_ge(x_r, r + 2)
                act.wait_ge(squared2, r + 1)
                nc.scalar.activation(junk2[:, :], tile_of(m.X, r), ACT.Square, accum_out=s2[:, 0:1]).then_inc(squared2, 1)
                act.wait_ge(meaned2, r + 1)
                nc.scalar.activation(s2[:, :], s2[:, :], ACT.Sqrt).then_inc(rooted2, 1)

            def route(r):
                act.wait_ge(turned2, r + 1)
                act.wait_ge(logits, r + 1)
                nc.scalar.activation(h2T[:, 0:4, :].rearrange("p k c -> p (k c)"), ps[4][:, :], ACT.Copy).then_inc(h2T_act, 1)
            staged(act, mix, update, route)

        @block.vector
        def _(dve):
            credit(dve, osum_r, on_r, mixed_r, turned, inverted, squared, squared2, prod, tmp_r, x_r, h2T_dve, logits, logits_r)
            dve.sem_inc(stored, 16)

            def prepare():
                dve.wait_ge(const, CONST)
                for v in range(vecs):
                    nc.vector.scalar_tensor_tensor(out=a2[:, v, :], in0=a2[:, v, :], scalar=1.0, in1=fw[:, :], op0=ALU.add,
                                                   op1=ALU.mult).then_inc(a2_r, 1)
                dve.wait_ge(a2_r, vecs)

            def mix(r):
                dve.wait_ge(squared, r + 2)
                nc.vector.tensor_scalar(ss[:, :], ss[:, :], 1.0 / P, EPS, ALU.mult, ALU.add).then_inc(meaned, 1)
                dve.wait_ge(rooted, r + 1)
                nc.vector.reciprocal(ss[:, :], ss[:, :]).then_inc(inverted, 1)
                dve.wait_ge(inverted, r + 2)
                dve.wait_ge(turned, r + 1)
                nc.vector.tensor_tensor(heads(mixed[:, :]), heads(osum[:, :]), over_cols(ss[:, :], NH), ALU.mult).then_inc(on_r, 1)
                dve.wait_ge(on_r, r + 2)
                dve.wait_ge(zn_r, r + 1)
                nc.vector.tensor_tensor(mixed[:, :], mixed[:, :], zn[:, :], ALU.mult).then_inc(mixed_r, 1)

            def take(r):
                dve.wait_ge(prod, r + 2)
                dve.wait_ge(x_r, r + 1)
                for half in range(2):
                    c = slice(half * HW, (half + 1) * HW)
                    a = nc.vector.tensor_tensor(tmp[:, c], ps[2 + half][:, :], g1[:, vec(r), c], ALU.mult)
                a.then_inc(tmp_r, 1)

            def update(r):
                dve.wait_ge(squared2, r + 2)
                nc.vector.tensor_scalar(s2[:, :], s2[:, :], 1.0 / D, EPS, ALU.mult, ALU.add).then_inc(meaned2, 1)
                dve.wait_ge(rooted2, r + 1)
                nc.vector.reciprocal(s2[:, :], s2[:, :]).then_inc(inverted2, 1)
                dve.wait_ge(inverted2, r + 1)
                dve.wait_ge(stored, r * 16 + 16)
                nc.vector.scalar_tensor_tensor(out=h2[:, :], in0=tile_of(m.X, r), scalar=s2[:, 0:1], in1=a2[:, vec(r), :],
                                               op0=ALU.mult, op1=ALU.mult).then_inc(xn_r, 1)

            def route(r):
                dve.wait_ge(turned2, r + 1)
                dve.wait_ge(logits, r + 1)
                nc.vector.tensor_copy(h2T[:, 4:8, :].rearrange("p k c -> p (k c)"), ps[5][:, :]).then_inc(h2T_dve, 1)
                dve.wait_ge(logits, r + 2)
                nc.vector.tensor_copy(tile_of(m.logits, r), ps[6][:, 0:NE]).then_inc(logits_r, 1)
            staged(dve, mix, update, route, take, prepare)

        @block.tensor
        def _(pe):
            def mix(r):
                pe.wait_ge(mixed_r, r + 2)
                pe.wait_ge(fst_r, r + 1)
                pe.wait_ge(mixT_r, r + 1)
                for half, src in enumerate((mixed, fst)):
                    for k in range(NH):
                        tr = nc.tensor.transpose(ps[half][:, k * P:(k + 1) * P], src[:, k * P:(k + 1) * P], m.ident[:, :])
                tr.then_inc(turned, 1)

            def update(r):
                pe.wait_ge(mixT_r, r + 2)
                pe.wait_ge(tmp_r, r + 1)
                for half in range(2):
                    for k in range(KD):
                        mm = nc.tensor.matmul(ps[2 + half][:, :], mixT[:, k, :], w_out[:, k, half * HW:(half + 1) * HW],
                                              start=(k == 0), stop=(k == KD - 1))
                mm.then_inc(prod, 1)

            def route(r):
                pe.wait_ge(h2_r, r + 1)
                pe.wait_ge(h2T_act, r + 1)
                pe.wait_ge(h2T_dve, r + 1)
                for k in range(KD):
                    tr = nc.tensor.transpose(ps[4 + k // 4][:, k % 4 * P:(k % 4 + 1) * P], h2[:, k * P:(k + 1) * P], m.ident[:, :])
                tr.then_inc(turned2, 1)
                pe.wait_ge(h2T_act, r + 2)
                pe.wait_ge(h2T_dve, r + 2)
                pe.wait_ge(logits_r, r + 1)
                for k in range(KD):
                    mm = nc.tensor.matmul(ps[6][:, 0:NE], h2T[:, k, :], rw[:, k, :], start=(k == 0), stop=(k == KD - 1))
                mm.then_inc(logits, 1)
            mix(0)
            pe.wait_ge(w_loaded, 32)
            update(0)
            mix(1)
            pe.wait_ge(const, CONST)
            with pe.Fori(0, NLT - 2) as q:
                update(q + 1)
                mix(q + 2)
                route(q)
            for r in range(NLT - 1, n):
                update(r)
                if r + 1 < n:
                    mix(r + 1)
                route(r - 1)
            route(n - 1)


def routing(nc, m, g, layer, first, n):
    stack, sb, banks, sem = phase(nc, f"route{layer}")
    NB = max_blocks(n * P)
    with stack:
        def t16(name):
            return sb(name, [P, n, NE])

        def t4(name):
            return sb(name, [P, n, NG])
        sc, bi, e1, e2, ma, M, SM, dm, sel = (t16(x) for x in ("sc", "bi", "e1", "e2", "ma", "M", "SM", "dm", "sel"))
        m1, m2, gsc, ge, seen = (t4(x) for x in ("m1", "m2", "gsc", "ge", "seen"))
        best = sb("best", [P, n])
        pre = sb("pre", [P, n + 1, NE])
        rb = sb("rb", [P, NE])
        cnt, cntf, pend, pend2, pstart = sb("cnt", [P, NE], I32), sb("cntf", [P, NE]), sb("pend", [P, NE]), sb("pend2", [P, NE]), sb("pstart", [P, NE])
        d0, d1, ssum = sb("d0", [P, n]), sb("d1", [P, n]), sb("ssum", [P, n])
        tok = sb("tok", [P, n], I32)
        starts = sb("starts", [1, NB, NE])
        over = sb("over", [1, NB, NE])
        bef = sb("bef", [1, NB])
        blk_e = sb("blk_e", [1, NB], I32)
        ends = sb("ends", [1, NE], I32)
        zero = sb("zero", [P, NB], I32)
        ps = banks(2)
        loaded, iotas, zeroed, exped, step, ranked, slotted, scattered, fetched = (
            sem(x) for x in ("loaded", "iotas", "zeroed", "exped", "step", "ranked", "slotted", "scattered", "fetched"))
        table, stepped = sem("table"), sem("stepped")
        block = stack.enter_context(nc.Block())

        @block.sync
        def _(sp):
            sp.dma_start(rb[:, :], g.router_bias.partition_broadcast(P)).then_inc(loaded, 16)
            sp.wait_ge(iotas, 3)
            sp.dma_start(g.slots[0:NB * P, :].rearrange("(p b) a -> p (b a)", p=P), zero[:, :]).then_inc(zeroed, 16)
            sp.wait_ge(zeroed, 16)
            sp.wait_ge(scattered, 32 * n)
            sp.dma_start(m.blk_tok[:, 0:NB], g.slots[0:NB * P, :].rearrange("(b p) a -> p (b a)", p=P),
                         allow_slow_non_contiguous=True).then_inc(fetched, 16)
            sp.wait_ge(fetched, 16)

        @block.gpsimd
        def _(pool):
            nc.gpsimd.iota(tok[:, :], pattern=[[P, n]], base=first * P, channel_multiplier=1).then_inc(iotas, 1)
            nc.gpsimd.memset(zero[:, :], 0).then_inc(iotas, 1)
            nc.gpsimd.memset(pre[:, 0, :], 0.0).then_inc(iotas, 1)
            pool.wait_ge(iotas, 3)
            pool.wait_ge(zeroed, 16)
            pool.wait_ge(slotted, 1)
            for t in range(n):
                for d in (m.d0i, m.d1i):
                    pool.indirect_dma_start(out=g.slots[0:NB * P, :], out_offset=bass.IndirectOffsetOnAxis(ap=d[:, t:t + 1], axis=0),
                                            in_=tok[:, t:t + 1], in_offset=None).then_inc(scattered, 16)
            pool.wait_ge(scattered, 32 * n)

        @block.scalar
        def _(act):
            act.dma_start(starts[:, :, :], g.block_starts[:, 0:NB, :]).then_inc(table, 16)
            nc.scalar.activation(sc[:, :, :], m.logits[:, first:first + n, :], ACT.Exp, scale=-1.0).then_inc(exped, 1)

        @block.tensor
        def _(pe):
            pe.wait_ge(stepped, 1)
            nc.tensor.matmul(ps[0][:, 0:n * NE], m.after[:, 1, :], M[:, :, :].rearrange("p t e -> p (t e)"), start=True, stop=False)
            nc.tensor.matmul(ps[0][:, 0:n * NE], m.ones[:, :], pre[:, 0:n, :].rearrange("p t e -> p (t e)"), start=False, stop=True)
            nc.tensor.matmul(ps[1][:, 0:NE], m.ones[:, :], pre[:, n, :], start=True, stop=True).then_inc(ranked, 1)

        @block.vector
        def _(dve):
            count = [0]

            def link(ins):
                count[0] += 1
                ins.then_inc(step, 1)
                dve.wait_ge(step, count[0])

            def tt(out, a, b, op):
                link(nc.vector.tensor_tensor(out, a, b, op))

            def over_group(ap):
                return ap.unsqueeze(3).broadcast_to([P, n, NG, EPG])

            def grp(t):
                return t[:, :, :].rearrange("p t (g e) -> p t g e", g=NG)

            def first_only(eq, size):
                link(nc.vector.tensor_copy(seen_of(eq), eq(0)))
                for j in range(1, size):
                    tt(eq(j), eq(j), seen_of(eq), ALU.is_gt)
                    if j < size - 1:
                        tt(seen_of(eq), seen_of(eq), eq(j), ALU.max)

            def seen_of(eq):
                return seen[:, :, :] if eq is not ge_at else seen[:, :, 0]

            def e1_at(j):
                return grp(e1)[:, :, :, j]

            def e2_at(j):
                return grp(e2)[:, :, :, j]

            def ge_at(j):
                return ge[:, :, j]
            dve.wait_ge(loaded, 16)
            dve.wait_ge(iotas, 3)
            dve.wait_ge(exped, 1)
            link(nc.vector.tensor_scalar(sc[:, :, :], sc[:, :, :], 1.0, None, ALU.add))
            link(nc.vector.reciprocal(sc[:, :, :], sc[:, :, :]))
            tt(bi[:, :, :], sc[:, :, :], rb[:, :].unsqueeze(1).broadcast_to([P, n, NE]), ALU.add)
            link(nc.vector.tensor_reduce(m1[:, :, :], grp(bi), X_AXIS, ALU.max))
            tt(grp(e1), grp(bi), over_group(m1[:, :, :]), ALU.is_equal)
            first_only(e1_at, EPG)
            link(nc.vector.scalar_tensor_tensor(out=ma[:, :, :].rearrange("p t e -> p (t e)"), in0=e1[:, :, :].rearrange("p t e -> p (t e)"),
                                                scalar=-1e30, in1=bi[:, :, :].rearrange("p t e -> p (t e)"), op0=ALU.mult, op1=ALU.add))
            link(nc.vector.tensor_reduce(m2[:, :, :], grp(ma), X_AXIS, ALU.max))
            tt(grp(e2), grp(ma), over_group(m2[:, :, :]), ALU.is_equal)
            first_only(e2_at, EPG)
            tt(gsc[:, :, :], m1[:, :, :], m2[:, :, :], ALU.add)
            link(nc.vector.tensor_reduce(best[:, :], gsc[:, :, :], X_AXIS, ALU.max))
            tt(ge[:, :, :], gsc[:, :, :], best[:, :].unsqueeze(2).broadcast_to([P, n, NG]), ALU.is_equal)
            first_only(ge_at, NG)
            tt(M[:, :, :], e1[:, :, :], e2[:, :, :], ALU.add)
            tt(grp(M), grp(M), over_group(ge[:, :, :]), ALU.mult)
            for t in range(n):
                tt(pre[:, t + 1, :], pre[:, t, :], M[:, t, :], ALU.add)
            nc.vector.tensor_tensor(SM[:, :, :], sc[:, :, :], M[:, :, :], ALU.mult).then_inc(stepped, 1)
            dve.wait_ge(stepped, 1)
            link(nc.vector.tensor_reduce(ssum[:, :], SM[:, :, :], X_AXIS, ALU.add))
            dve.wait_ge(ranked, 1)
            link(nc.vector.tensor_scalar(cnt[:, :], ps[1][:, 0:NE], float(P - 1), None, ALU.add))
            link(nc.vector.tensor_scalar(cnt[:, :], cnt[:, :], 7, 7, ALU.arith_shift_right, ALU.arith_shift_left))
            link(nc.vector.tensor_copy(cntf[:, :], cnt[:, :]))
            link(nc.vector.tensor_copy(pend[:, :], cntf[:, :]))
            a, b = pend, pend2
            for s in (1, 2, 4, 8):
                link(nc.vector.tensor_copy(b[:, 0:s], a[:, 0:s]))
                tt(b[:, s:NE], a[:, s:NE], a[:, 0:NE - s], ALU.add)
                a, b = b, a
            tt(pstart[:, :], a[:, :], cntf[:, :], ALU.subtract)
            tt(dm[:, :, :], ps[0][:, 0:n * NE].rearrange("p (t e) -> p t e", t=n), pstart[:, :].unsqueeze(1).broadcast_to([P, n, NE]), ALU.add)
            tt(dm[:, :, :], dm[:, :, :], M[:, :, :], ALU.mult)
            link(nc.vector.tensor_reduce(d1[:, :], dm[:, :, :], X_AXIS, ALU.max))
            link(nc.vector.tensor_reduce(d0[:, :], dm[:, :, :], X_AXIS, ALU.add))
            tt(d0[:, :], d0[:, :], d1[:, :], ALU.subtract)
            link(nc.vector.tensor_copy(m.d0i[:, 0:n], d0[:, :]))
            nc.vector.tensor_copy(m.d1i[:, 0:n], d1[:, :]).then_inc(slotted, 1)
            tt(sel[:, :, :], dm[:, :, :], d1[:, :].unsqueeze(2).broadcast_to([P, n, NE]), ALU.is_equal)
            tt(sel[:, :, :], sel[:, :, :], SM[:, :, :], ALU.mult)
            link(nc.vector.tensor_reduce(m.w1[:, 0:n], sel[:, :, :], X_AXIS, ALU.add))
            tt(m.w0[:, 0:n], ssum[:, :], m.w1[:, 0:n], ALU.subtract)
            link(nc.vector.reciprocal(ssum[:, :], ssum[:, :]))
            tt(m.w0[:, 0:n], m.w0[:, 0:n], ssum[:, :], ALU.mult)
            tt(m.w1[:, 0:n], m.w1[:, 0:n], ssum[:, :], ALU.mult)
            dve.wait_ge(table, 16)
            tt(over[:, :, :], a[0:1, :].unsqueeze(1).broadcast_to([1, NB, NE]), starts[:, :, :], ALU.is_le)
            link(nc.vector.tensor_reduce(bef[:, :], over[:, :, :], X_AXIS, ALU.add))
            link(nc.vector.tensor_scalar(blk_e[:, :], bef[:, :], float(NE - 1), None, ALU.min))
            link(nc.vector.tensor_scalar(m.buffer[:, 0:NB], blk_e[:, :], 1, None, ALU.bitwise_and))
            link(nc.vector.tensor_scalar(m.loads0[:, 0:NB], blk_e[:, :], 1, 4, ALU.arith_shift_right, ALU.arith_shift_left))
            tt(m.loads1[:, 0:NB], blk_e[:, :], m.buffer[:, 0:NB], ALU.add)
            link(nc.vector.tensor_scalar(m.loads1[:, 0:NB], m.loads1[:, 0:NB], 1, 4, ALU.arith_shift_right, ALU.arith_shift_left))
            for t in (m.loads0, m.loads1):
                link(nc.vector.tensor_scalar(t[:, 0:NB], t[:, 0:NB], 16, None, ALU.add))
            link(nc.vector.tensor_copy(ends[:, :], a[0:1, :]))
            for t, plus in ((m.even, 1), (m.odd, 0)):
                link(nc.vector.memset(t[:, 0:2], 1))
                link(nc.vector.tensor_scalar(t[:, 2:NE + 2], ends[:, :], plus * P, None, ALU.add))
                link(nc.vector.tensor_scalar(t[:, 2:NE + 2], t[:, 2:NE + 2], 8, None, ALU.arith_shift_right))
                link(nc.vector.tensor_scalar(t[:, 2:NE + 2], t[:, 2:NE + 2], 1, None, ALU.add))
            link(nc.vector.tensor_scalar(m.pairs_but_one[:, :], m.even[:, NE + 1:NE + 2], -2, None, ALU.add))


def experts(nc, m, g, layer, n):
    stack, sb, banks, sem = phase(nc, f"moe{layer}")
    NB = max_blocks(n * P)
    with stack:
        wg = sb("wg", [P, 2, KD, DE])
        wu = sb("wu", [P, 2, KD, DE])
        wd = sb("wd", [P, 2, KE, D])
        idx = sb("idx", [P, 2], U32)
        xg = sb("xg", [P, 2, D])
        xT = sb("xT", [P, 2, KD, P])
        sg, hid = sb("sg", [P, DE]), sb("hid", [P, DE])
        hT = sb("hT", [P, KE, P])
        ys = sb("ys", [P, 2, D])
        ps = banks(7)

        def pair(name):
            return [sem(f"{name}0"), sem(f"{name}1")]
        g_loaded, u_loaded, d_loaded, gathered, picked, turned_a, turned_b, xT_act, xT_dve, gu, down, y_act, y_dve, stored = (
            pair(x) for x in ("g_loaded", "u_loaded", "d_loaded", "gathered", "picked", "turned_a", "turned_b", "xT_act",
                              "xT_dve", "gu", "down", "y_act", "y_dve", "stored"))
        gate = sem("gate")

        def pairs_but_one(eng):
            return eng.value_load(m.pairs_but_one[0:1, 0:1], min_val=n - 1, max_val=NB // 2 - 1)
        issued = pair("issued")
        load_turns = sem("load_turns")
        all_stored = sem("all_stored")
        sg_r, hid_r, hid_turned, hT_r = (sem(x) for x in ("sg", "hid", "hid_turned", "hT"))
        block = stack.enter_context(nc.Block())

        @block.sync
        def _(sp):
            def load(j, e, i):
                even = sp.value_load(m.even[0:1, bass.ds(e, 1)], min_val=1, max_val=NB)
                odd = sp.value_load(m.odd[0:1, bass.ds(e, 1)], min_val=1, max_val=NB)
                sp.wait_ge(gu[0], even)
                sp.wait_ge(gu[1], odd)
                for s in (g_loaded[j], u_loaded[j], d_loaded[j]):
                    sp.sem_inc(load_turns, 1)
                    sp.wait_ge(s, i * 16 + 16 * j)
                sp.sem_inc(load_turns, 1)
                sp.dma_start(wg[:, j, :, :], g.w_gate[layer][bass.ds(e, 1), :, :].rearrange("e (k p) n -> p (e k) n", p=P)).then_inc(g_loaded[j], 16)
                sp.dma_start(wu[:, j, :, :], g.w_up[layer][bass.ds(e, 1), :, :].rearrange("e (k p) n -> p (e k) n", p=P)).then_inc(u_loaded[j], 16)
                sp.wait_ge(down[0], even)
                sp.wait_ge(down[1], odd)
                sp.sem_inc(load_turns, 1)
                sp.dma_start(wd[:, j, :, :], g.w_down[layer][bass.ds(e, 1), :, :].rearrange("e (k p) n -> p (e k) n", p=P)).then_inc(d_loaded[j], 16)
            with sp.Fori(0, NE // 2) as i:
                for j in range(2):
                    load(j, i * 2 + j, i)

        @block.gpsimd
        def _(pool):
            full = pairs_but_one(pool)
            with pool.Fori(0, full + 1) as i:
                for j in range(2):
                    pool.wait_ge(turned_b[j], i + 1)
                    nc.gpsimd.tensor_copy(idx[:, j:j + 1], m.blk_tok[:, bass.ds(i * 2 + j, 1)]).then_inc(picked[j], 1)
                    pool.wait_ge(picked[j], i + 1)
                    pool.sem_inc(issued[j], 1)
                    pool.indirect_dma_start(out=xg[:, j, :], out_offset=None, in_=g.h2[:, :],
                                            in_offset=bass.IndirectOffsetOnAxis(ap=idx[:, j:j + 1], axis=0)).then_inc(gathered[j], 16)

        def blocks(eng, body, lead):
            lead(0, 0)
            full = pairs_but_one(eng)
            with eng.Fori(0, full) as i:
                body(0, i, i * 2, (1, i))
                body(1, i, i * 2 + 1, (0, i + 1))
            body(0, full, full * 2, (1, full))
            body(1, full, full * 2 + 1, None)

        @block.tensor
        def _(pe):
            def turn_half(j, i, half):
                if half == 0:
                    pe.wait_ge(gathered[j], i * 16 + 16)
                pe.wait_ge((xT_act, xT_dve)[half][1 - j], i + 1 + (j == 1))
                for k in range(4):
                    tr = nc.tensor.transpose(ps[2 + half][:, k * P:(k + 1) * P], xg[:, j, (half * 4 + k) * P:(half * 4 + k + 1) * P],
                                             m.ident[:, :])
                tr.then_inc((turned_a, turned_b)[half][j], 1)

            def lead(j, i):
                turn_half(j, i, 0)
                turn_half(j, i, 1)

            def body(j, i, b, following):
                buffer = pe.value_load(m.buffer[0:1, bass.ds(b, 1)], min_val=0, max_val=1)
                loads = [pe.value_load(t[0:1, bass.ds(b, 1)], min_val=16, max_val=16 * (NE // 2 + 1)) for t in (m.loads0, m.loads1)]

                def arrived(sems):
                    for s, count in zip(sems, loads):
                        pe.wait_ge(s, count)

                def weights(w, k, cols):
                    return w[:, bass.ds(buffer, 1), k, cols].rearrange("p a n -> p (a n)")
                pe.wait_ge(xT_act[j], i + 2)
                pe.wait_ge(xT_dve[j], i + 2)
                pe.wait_ge(hid_r, b + 1)
                for bank, w, sems, done in ((0, wg, g_loaded, gate), (1, wu, u_loaded, gu[j])):
                    arrived(sems)
                    for k in range(KD):
                        mm = nc.tensor.matmul(ps[bank][:, :], xT[:, j, k, :], weights(w, k, slice(0, DE)), start=(k == 0), stop=(k == KD - 1))
                    mm.then_inc(done, 1)
                if following:
                    turn_half(*following, 0)
                pe.wait_ge(hid_r, b + 2)
                pe.wait_ge(hT_r, b + 1)
                for k in range(KE):
                    tr = nc.tensor.transpose(ps[4][:, k * P:(k + 1) * P], hid[:, k * P:(k + 1) * P], m.ident[:, :])
                tr.then_inc(hid_turned, 1)
                if following:
                    turn_half(*following, 1)
                arrived(d_loaded)
                pe.wait_ge(hT_r, b + 2)
                pe.wait_ge(y_act[1 - j], i + 1 + j)
                pe.wait_ge(y_dve[1 - j], i + 1 + j)
                for half in range(2):
                    for k in range(KE):
                        mm = nc.tensor.matmul(ps[5 + half][:, :], hT[:, k, :], weights(wd, k, slice(half * DE, (half + 1) * DE)),
                                              start=(k == 0), stop=(k == KE - 1))
                mm.then_inc(down[j], 1)
            blocks(pe, body, lead)

        @block.scalar
        def _(act):
            credit(act, *xT_act, *xT_dve, hid_r, hT_r, *gu, *down, *turned_b, *y_act, *y_dve)
            for s in (*stored, g_loaded[1], u_loaded[1], d_loaded[1]):
                act.sem_inc(s, 16)

            def evacuate(j, i):
                act.wait_ge(turned_a[j], i + 1)
                act.wait_ge(gu[j], i + 1)
                nc.scalar.activation(xT[:, j, 0:4, :].rearrange("p k c -> p (k c)"), ps[2][:, :], ACT.Copy).then_inc(xT_act[j], 1)

            def body(j, i, b, following):
                act.wait_ge(gate, b + 1)
                act.wait_ge(hid_r, b + 1)
                nc.scalar.activation(sg[:, :], ps[0][:, :], ACT.Silu).then_inc(sg_r, 1)
                if following:
                    evacuate(*following)
                act.wait_ge(hid_turned, b + 1)
                nc.scalar.activation(hT[:, :, :].rearrange("p k c -> p (k c)"), ps[4][:, :], ACT.Copy).then_inc(hT_r, 1)
                act.wait_ge(down[j], i + 2)
                act.wait_ge(stored[j], i * 16 + 16)
                nc.scalar.activation(ys[:, j, 0:DE], ps[5][:, :], ACT.Copy).then_inc(y_act[j], 1)
                act.wait_ge(y_act[j], i + 2)
                act.wait_ge(y_dve[j], i + 2)
                act.dma_start(g.ys[bass.ds(b * P, P), :], ys[:, j, :]).then_inc(stored[j], 16)
            blocks(act, body, evacuate)
            full = pairs_but_one(act)
            for s in stored:
                act.wait_ge(s, full * 16 + 32)
                act.sem_inc(all_stored, 1)

        @block.vector
        def _(dve):
            def evacuate(j, i):
                dve.wait_ge(turned_b[j], i + 2)
                dve.wait_ge(gu[j], i + 1)
                nc.vector.tensor_copy(xT[:, j, 4:8, :].rearrange("p k c -> p (k c)"), ps[3][:, :]).then_inc(xT_dve[j], 1)

            def body(j, i, b, following):
                dve.wait_ge(gu[j], i + 2)
                dve.wait_ge(sg_r, b + 1)
                nc.vector.tensor_tensor(hid[:, :], sg[:, :], ps[1][:, :], ALU.mult).then_inc(hid_r, 1)
                if following:
                    evacuate(*following)
                dve.wait_ge(down[j], i + 2)
                dve.wait_ge(stored[j], i * 16 + 16)
                nc.vector.tensor_copy(ys[:, j, DE:D], ps[6][:, :]).then_inc(y_dve[j], 1)
            blocks(dve, body, evacuate)


def combine(nc, m, g, layer, first, n, out):
    stack, sb, banks, sem = phase(nc, f"comb{layer}")
    last = out is not None
    with stack:
        g2 = sb("g2", [P, 2, D])
        idx = sb("idx", [P, 2, 2], U32)
        y = sb("y", [P, 2, 2, D])
        w = sb("w", [P, 2, 2])
        acc = sb("acc", [P, 2, D])
        fw = sb("fw", [P, D])
        s2 = sb("s2", [P, 2])
        res = sb("res", [P, 2, D])

        def pair(name):
            return [sem(f"{name}0"), sem(f"{name}1")]
        picked, gathered, scaled, summed, gated, added, w_r, squared, meaned, rooted, inverted, normed, stored = (
            pair(x) for x in ("picked", "gathered", "scaled", "summed", "gated", "added", "w", "squared", "meaned", "rooted",
                              "inverted", "normed", "stored"))
        const = sem("const")
        issued = pair("issued")
        mod = None if last else Modulation(nc, m, g, layer + 1, sb, banks(3), sem)
        block = stack.enter_context(nc.Block())
        NR = n // 2

        def tile_of(t, r):
            return t[:, bass.ds(r, 1), :].rearrange("p a n -> p (a n)")

        @block.sync
        def _(sp):
            for v in range(2):
                sp.dma_start(g2[:, v, :], g.mods[layer, v, 5 * D:6 * D].partition_broadcast(P)).then_inc(const, 16)
            sp.dma_start(fw[:, :], g.final_norm_w.partition_broadcast(P)).then_inc(const, 16)
            if last:
                with sp.Fori(0, NR) as i:
                    for j in range(2):
                        sp.wait_ge(normed[j], i + 1)
                        sp.dma_start(out[bass.ds((i * 2 + j) * P, P), :], res[:, j, :]).then_inc(stored[j], 16)
                for j in range(2):
                    sp.wait_ge(stored[j], 16 * (NR + 1))
            else:
                mod.load(sp)
                mod.store(sp)

        @block.gpsimd
        def _(pool):
            with pool.Fori(0, NR) as i:
                for j in range(2):
                    pool.wait_ge(summed[j], i + 1)
                    nc.gpsimd.tensor_copy(idx[:, j, 0:1], m.d0i[:, bass.ds(i * 2 + j, 1)]).then_inc(picked[j], 1)
                    nc.gpsimd.tensor_copy(idx[:, j, 1:2], m.d1i[:, bass.ds(i * 2 + j, 1)]).then_inc(picked[j], 1)
                    pool.wait_ge(picked[j], i * 2 + 2)
                    pool.sem_inc(issued[j], 1)
                    for s in range(2):
                        pool.indirect_dma_start(out=y[:, j, s, :], out_offset=None, in_=g.ys[:, :],
                                                in_offset=bass.IndirectOffsetOnAxis(ap=idx[:, j, s:s + 1], axis=0)).then_inc(gathered[j], 16)

        @block.vector
        def _(dve):
            credit(dve, *summed)
            for j in range(2):
                dve.sem_inc(stored[j], 16)
            dve.wait_ge(const, 48)

            def tile(j, i, vec):
                r = i * 2 + j
                nc.vector.tensor_copy(w[:, j, 0:1], m.w0[:, bass.ds(r, 1)]).then_inc(w_r[j], 1)
                nc.vector.tensor_copy(w[:, j, 1:2], m.w1[:, bass.ds(r, 1)]).then_inc(w_r[j], 1)
                dve.wait_ge(w_r[j], i * 2 + 2)
                dve.wait_ge(gathered[j], i * 32 + 32)
                nc.vector.tensor_scalar(acc[:, j, :], y[:, j, 0, :], w[:, j, 0:1], None, ALU.mult).then_inc(scaled[j], 1)
                dve.wait_ge(scaled[j], i + 1)
                nc.vector.scalar_tensor_tensor(out=acc[:, j, :], in0=y[:, j, 1, :], scalar=w[:, j, 1:2], in1=acc[:, j, :],
                                               op0=ALU.mult, op1=ALU.add).then_inc(summed[j], 1)
                dve.wait_ge(summed[j], i + 2)
                nc.vector.tensor_tensor(acc[:, j, :], acc[:, j, :], g2[:, vec, :], ALU.mult).then_inc(gated[j], 1)
                dve.wait_ge(gated[j], i + 1)
                nc.vector.tensor_tensor(tile_of(m.X, r + first), tile_of(m.X, r + first), acc[:, j, :], ALU.add).then_inc(added[j], 1)

            def norm(j, i):
                r = i * 2 + j
                dve.wait_ge(squared[j], i + 1)
                nc.vector.tensor_scalar(s2[:, j:j + 1], s2[:, j:j + 1], 1.0 / D, EPS, ALU.mult, ALU.add).then_inc(meaned[j], 1)
                dve.wait_ge(rooted[j], i + 1)
                nc.vector.reciprocal(s2[:, j:j + 1], s2[:, j:j + 1]).then_inc(inverted[j], 1)
                dve.wait_ge(inverted[j], i + 1)
                dve.wait_ge(stored[j], i * 16 + 16)
                nc.vector.scalar_tensor_tensor(out=res[:, j, :], in0=tile_of(m.X, r + first), scalar=s2[:, j:j + 1], in1=fw[:, :],
                                               op0=ALU.mult, op1=ALU.mult).then_inc(normed[j], 1)
            start = 0
            if first == 0:
                for j in range(NCT):
                    tile(j, 0, CTXV)
                start = 1
            with dve.Fori(start, NR) as i:
                for j in range(2):
                    tile(j, i, LAT)
                if last:
                    for j in range(2):
                        norm(j, i)
            if not last:
                mod.finish(dve)

        if not last:
            @block.tensor
            def _(pe):
                mod.products(pe)
                mod.turn(pe)

        @block.scalar
        def _(act):
            if not last:
                mod.load_small(act)
                mod.take(act)
            else:
                with act.Fori(0, NR) as i:
                    for j in range(2):
                        act.wait_ge(added[j], i + 1)
                        nc.scalar.activation(acc[:, j, :], tile_of(m.X, i * 2 + j + first), ACT.Square,
                                             accum_out=s2[:, j:j + 1]).then_inc(squared[j], 1)
                        act.wait_ge(meaned[j], i + 1)
                        nc.scalar.activation(s2[:, j:j + 1], s2[:, j:j + 1], ACT.Sqrt).then_inc(rooted[j], 1)


class Globals:
    pass


def program(nc, g, out, stop=None):
    stack = ExitStack()
    with stack:
        m = Memory(nc, stack)
        load_start(nc, m, g)
        for layer in range(DEPTH):
            with ExitStack() as mix:
                def sb(name, shape):
                    return mix.enter_context(nc.sbuf_tensor(f"{name}{layer}", shape, F32))
                m.Z = sb("Z", [P, NT, HW])
                m.AB = sb("AB", [P, NT, 4 * NH])
                with ExitStack() as early:
                    m.hT = early.enter_context(nc.sbuf_tensor(f"hT{layer}", [P, KD, NT * P], F32))
                    token_projections(nc, m, g, layer)
                    if stop == "tok":
                        return dump(nc, m, g, out)
                    feature_projections(nc, m, g, layer)
                    if stop == "feat":
                        return dump(nc, m, g, out)
                m.F = sb("F", [P, NT, HW])
                fourier(nc, m, g, layer, layer == DEPTH - 1)
                if stop == "four":
                    return dump(nc, m, g, out)
                delta(nc, m, g, layer)
                if stop == "delta":
                    return dump(nc, m, g, out)
                first = 0 if layer < DEPTH - 1 else NCT
                n = NT - first
                output_projection(nc, m, g, layer, n)
                if stop == "out":
                    return dump(nc, m, g, out)
            routing(nc, m, g, layer, first, n)
            if stop == "route":
                return dump(nc, m, g, out)
            experts(nc, m, g, layer, n)
            combine(nc, m, g, layer, first, n, out if layer == DEPTH - 1 and stop is None else None)
            if stop == f"layer{layer}":
                return dump(nc, m, g, out)


def dump(nc, m, g, out):
    with nc.semaphore("dumped") as s, nc.Block() as block:
        @block.sync
        def _(sp):
            n = 0
            for o, src in zip(out, g.dump(m)):
                sp.dma_start(o, src).then_inc(s, 16)
                n += 16
            sp.wait_ge(s, n)


SCRATCH = {"mods": ([DEPTH, 2, MODS], F32), "dft1": ([NT, P, 2 * HW], F32),
           "qkv": ([3 * NH, P, CHUNK_POS * P], F32), "o": ([2, CHUNK_POS, P, HW], F32),
           "h2": ([NT * P, D], F32), "slots": ([max_blocks(NT * P) * P, 1], I32), "ys": ([max_blocks(NT * P) * P, D], F32)}
INPUTS = ["x", "ctx", "ada_w", "ada_b", "norm_ffn_w", "w_in", "a_log", "dt_bias",
          "dn_norm_w", "ft_norm_w", "w_out", "router_w", "router_bias", "w_gate", "w_up", "w_down", "final_norm_w"]


def columns(inputs):
    import numpy as np
    a = {n: np.asarray(inputs[n]) for n in ("c", "c_ctx", "norm_mix_w", "conv_w")}
    return {"c_cols": np.stack([a["c"][0], a["c_ctx"]]).reshape(2, KD, P).transpose(2, 0, 1),
            "norm_mix_cols": a["norm_mix_w"].reshape(DEPTH, KD, P).transpose(0, 2, 1),
            "conv_cols": a["conv_w"].reshape(DEPTH, CONV_K, 3 * NH, P).transpose(0, 3, 2, 1)}


def constants():
    import numpy as np
    i = np.arange(P)
    t, j = i[:, None], i[None, :]
    upto = np.stack([t <= j, t >= j], 1)
    after = np.stack([t > j, t < j], 1)
    lev = []
    for d in range(2):
        for l in range(LEVELS):
            s = 1 << l
            same = (t // (2 * s)) == (j // (2 * s))
            low = (t // s % 2 == 1) & (j // s % 2 == 0)
            high = (t // s % 2 == 0) & (j // s % 2 == 1)
            lev.append(same & (low if d == 0 else high))
    ang = 2 * np.pi * (t * j % P) / P
    cdsd = np.concatenate([np.cos(ang), np.sin(ang)], 1) / np.sqrt(P)
    consts = np.concatenate([np.eye(P), upto.reshape(P, -1), after.reshape(P, -1), np.ones((P, P)), cdsd,
                             np.stack(lev, 1).reshape(P, -1)], 1).astype(np.float32)

    def seq(n):
        k = np.arange(n)
        a = 2 * np.pi * (k[:, None] * k[None, :] % n) / n
        return (np.concatenate([np.cos(a), -np.sin(a)], 0) / np.sqrt(n)).astype(np.float32)

    quarter, width = D // 4, 64
    omega = (1.0 / (10000.0 ** (np.arange(quarter, dtype=np.float32) / quarter))).astype(np.float32)

    def emb(n):
        a = (np.arange(n, dtype=np.float32)[:, None] * omega).astype(np.float32)
        return np.concatenate([np.sin(a), np.cos(a)], 1).astype(np.float32)
    col = emb(width)
    nb = max_blocks(NT * P)
    starts = np.repeat(np.arange(nb, dtype=np.float32)[:, None] * P, NE, 1)[None]
    return {"block_starts": starts, "consts": consts, "dft_lat": seq(SEQ), "dft_ctx": seq(CTX), "emb_row": emb(SEQ // width),
            "emb_col": np.concatenate([col, col], 0)}


def kernel(**inputs):
    import numpy as np
    import concourse.bacc as bacc
    from concourse.bass_utils import run_bass_kernel_spmd as run

    nc = bacc.Bacc("TRN2", target_bir_lowering=False, num_devices=1)
    arrays, g = {}, Globals()
    for name, a in list((n, inputs[n]) for n in INPUTS) + list(columns(inputs).items()) + list(constants().items()):
        a = np.ascontiguousarray(a)
        arrays[f"in_{name}"] = a
        g.__dict__[name] = nc.dram_tensor(f"in_{name}", a.shape, mybir.dt.from_np(a.dtype), kind="ExternalInput").ap()
    for name, (shape, dt) in SCRATCH.items():
        g.__dict__[name] = nc.dram_tensor(f"scratch_{name}", shape, dt, kind="Internal").ap()
    out = nc.dram_tensor("out_0", (1, SEQ, D), F32, kind="ExternalOutput").ap()
    program(nc, g, out[0])
    return run(nc, [arrays], core_ids=[0]).results[0]["out_0"]
```
